# Optimizing a Trainium2 kernel written in Bass

```python
import math
import jax, jax.numpy as jnp
from jax import lax
import numpy as np

D_MODEL = 1024
BATCH = 1
SEQ = 512
DEPTH = 2

CHUNK = 64
N_META = 16
Q_BLOCK = 128
EPS = 1e-5

N_A_LAYERS = DEPTH // 2
N_B_LAYERS = DEPTH - N_A_LAYERS

DIFF_HEAD_DIM = 64
DIFF_HEADS = D_MODEL // (2 * DIFF_HEAD_DIM)
DIFF_V_DIM = 2 * DIFF_HEAD_DIM
ROPE_THETA = 500000.0
ROT_DIM = DIFF_HEAD_DIM // 4

MLA_HEADS = D_MODEL // 64
MLA_NOPE = 64
MLA_ROPE = 32
MLA_V = 64
Q_LORA = 3 * D_MODEL // 8
KV_LORA = D_MODEL // 4
MLA_ROPE_THETA = 10000.0

D_FF = 128 * ((8 * D_MODEL // 3 + 127) // 128)
CONV_W = 3


def rms_norm(x, g):
    xf = x.astype(jnp.float32)
    y = xf * lax.rsqrt(jnp.mean(xf * xf, axis=-1, keepdims=True) + EPS)
    return (y * g.astype(jnp.float32)).astype(x.dtype)

def rotary(x, pos, theta, rot_dim):
    half = rot_dim // 2
    inv = 1.0 / (theta ** (jnp.arange(half, dtype=jnp.float32) / half))
    ang = pos.astype(jnp.float32)[:, None] * inv[None, :]
    cos = jnp.cos(ang)[None, :, None, :]
    sin = jnp.sin(ang)[None, :, None, :]
    xr = x[..., :rot_dim].astype(jnp.float32)
    x1, x2 = xr[..., :half], xr[..., half:]
    rot = jnp.concatenate([x1 * cos - x2 * sin, x2 * cos + x1 * sin], axis=-1).astype(x.dtype)
    return jnp.concatenate([rot, x[..., rot_dim:]], axis=-1)

def chunk_ids(pos):
    return jnp.where(pos < N_META, 0, 1 + (pos - N_META) // CHUNK)

def to_query_blocks(q, n_blocks):
    B, L, H, d = q.shape
    q = jnp.pad(q, ((0, 0), (0, n_blocks * Q_BLOCK - L), (0, 0), (0, 0)))
    return q.reshape(B, n_blocks, Q_BLOCK, H, d).transpose(1, 0, 2, 3, 4)

def from_query_blocks(o, L):
    nb, B, qb, H, d = o.shape
    return o.transpose(1, 0, 2, 3, 4).reshape(B, nb * qb, H, d)[:, :L]

def diff_attention(q1, q2, k1, k2, v, lam, q_chunk_blocks, k_chunk):
    L = k1.shape[1]
    nb = q_chunk_blocks.shape[0]
    scale = DIFF_HEAD_DIM ** -0.5

    def block(args):
        qb1, qb2, qc = args
        mask = k_chunk[None, :] <= qc[:, None]

        def probs(qb, k):
            s = jnp.einsum('bqhd,bkhd->bhqk', qb, k).astype(jnp.float32) * scale
            return jax.nn.softmax(jnp.where(mask, s, -jnp.inf), axis=-1)

        a = probs(qb1, k1) - lam * probs(qb2, k2)
        return jnp.einsum('bhqk,bkhd->bqhd', a.astype(v.dtype), v)

    o = lax.map(block, (to_query_blocks(q1, nb), to_query_blocks(q2, nb), q_chunk_blocks))
    return from_query_blocks(o, L)

def mla_attention(q_nope, q_rope, k_nope, k_rope, v, q_chunk_blocks, k_chunk):
    L = k_nope.shape[1]
    nb = q_chunk_blocks.shape[0]
    scale = (MLA_NOPE + MLA_ROPE) ** -0.5

    def block(args):
        qn, qr, qc = args
        mask = k_chunk[None, :] <= qc[:, None]
        s = (jnp.einsum('bqhd,bkhd->bhqk', qn, k_nope)
             + jnp.einsum('bqhr,bkr->bhqk', qr, k_rope)).astype(jnp.float32) * scale
        p = jax.nn.softmax(jnp.where(mask, s, -jnp.inf), axis=-1)
        return jnp.einsum('bhqk,bkhd->bqhd', p.astype(v.dtype), v)

    o = lax.map(block, (to_query_blocks(q_nope, nb), to_query_blocks(q_rope, nb), q_chunk_blocks))
    return from_query_blocks(o, L)

def diff_attn_layer(h, g_norm, w_qkv, lq1, lk1, lq2, lk2, g_sub, w_o, layer_idx, pos, qcb, kc):
    B, L, _ = h.shape
    H, d = DIFF_HEADS, DIFF_HEAD_DIM
    xn = rms_norm(h, g_norm)
    qkv = xn @ w_qkv
    q, k, v = jnp.split(qkv, [2 * H * d, 4 * H * d], axis=-1)
    q = rotary(q.reshape(B, L, 2 * H, d), pos, ROPE_THETA, ROT_DIM).reshape(B, L, H, 2, d)
    k = rotary(k.reshape(B, L, 2 * H, d), pos, ROPE_THETA, ROT_DIM).reshape(B, L, H, 2, d)
    v = v.reshape(B, L, H, DIFF_V_DIM)
    lam_init = 0.8 - 0.6 * math.exp(-0.3 * layer_idx)
    lam = (jnp.exp(jnp.sum(lq1.astype(jnp.float32) * lk1.astype(jnp.float32)))
           - jnp.exp(jnp.sum(lq2.astype(jnp.float32) * lk2.astype(jnp.float32))) + lam_init)
    o = diff_attention(q[..., 0, :], q[..., 1, :], k[..., 0, :], k[..., 1, :], v, lam, qcb, kc)
    o = rms_norm(o, g_sub) * (1.0 - lam_init)
    return h + o.reshape(B, L, H * DIFF_V_DIM) @ w_o

def shared_latent_kv(h, g_norm, w_dkv, g_kv, w_ukv, pos):
    B, L, _ = h.shape
    xn = rms_norm(h, g_norm)
    ckv = xn @ w_dkv
    c_kv = rms_norm(ckv[..., :KV_LORA], g_kv)
    k_rope = rotary(ckv[..., None, KV_LORA:], pos, MLA_ROPE_THETA, MLA_ROPE)[:, :, 0]
    kv = (c_kv @ w_ukv).reshape(B, L, MLA_HEADS, MLA_NOPE + MLA_V)
    return kv[..., :MLA_NOPE], k_rope, kv[..., MLA_NOPE:]

def mla_layer(h, g_norm, w_dq, g_q, w_uq, w_o, k_nope, k_rope, v, pos, qcb, kc):
    B, L, _ = h.shape
    xn = rms_norm(h, g_norm)
    c_q = rms_norm(xn @ w_dq, g_q)
    q = (c_q @ w_uq).reshape(B, L, MLA_HEADS, MLA_NOPE + MLA_ROPE)
    q_nope = q[..., :MLA_NOPE]
    q_rope = rotary(q[..., MLA_NOPE:], pos, MLA_ROPE_THETA, MLA_ROPE)
    o = mla_attention(q_nope, q_rope, k_nope, k_rope, v, qcb, kc)
    return h + o.reshape(B, L, MLA_HEADS * MLA_V) @ w_o

def conv_ffn(h, g_norm, w_in, conv_w, conv_b, w_out):
    L = h.shape[1]
    xn = rms_norm(h, g_norm)
    a, b = jnp.split(xn @ w_in, 2, axis=-1)
    ap = jnp.pad(a, ((0, 0), (CONV_W - 1, 0), (0, 0)))
    a_conv = conv_b
    for j in range(CONV_W):
        a_conv = a_conv + ap[:, j:j + L] * conv_w[j]
    return h + (jax.nn.silu(a_conv) * b) @ w_out

def first_inputs(seed: int = 0) -> dict:
    key = jax.random.key(seed)
    ks = iter(jax.random.split(key, 32))
    f32 = jnp.float32

    def nrm(shape, scale):
        return jax.random.normal(next(ks), shape, f32) * scale

    def gain(shape):
        return 1.0 + 0.02 * jax.random.normal(next(ks), shape, f32)

    nA, nB = N_A_LAYERS, N_B_LAYERS
    qkv_out = 4 * DIFF_HEADS * DIFF_HEAD_DIM + DIFF_HEADS * DIFF_V_DIM
    return {
        "x": nrm((BATCH, SEQ, D_MODEL), 1.0),
        "meta_tokens": nrm((N_META, D_MODEL), 1.0),
        "a_attn_norm": gain((nA, D_MODEL)),
        "a_w_qkv": nrm((nA, D_MODEL, qkv_out), D_MODEL ** -0.5),
        "a_lambda_q1": nrm((nA, DIFF_HEAD_DIM), 0.1),
        "a_lambda_k1": nrm((nA, DIFF_HEAD_DIM), 0.1),
        "a_lambda_q2": nrm((nA, DIFF_HEAD_DIM), 0.1),
        "a_lambda_k2": nrm((nA, DIFF_HEAD_DIM), 0.1),
        "a_sub_norm": gain((nA, DIFF_V_DIM)),
        "a_w_o": nrm((nA, DIFF_HEADS * DIFF_V_DIM, D_MODEL), (DIFF_HEADS * DIFF_V_DIM) ** -0.5),
        "kv_norm": gain((D_MODEL,)),
        "kv_w_dkv": nrm((D_MODEL, KV_LORA + MLA_ROPE), D_MODEL ** -0.5),
        "kv_a_norm": gain((KV_LORA,)),
        "kv_w_ukv": nrm((KV_LORA, MLA_HEADS * (MLA_NOPE + MLA_V)), KV_LORA ** -0.5),
        "b_attn_norm": gain((nB, D_MODEL)),
        "b_w_dq": nrm((nB, D_MODEL, Q_LORA), D_MODEL ** -0.5),
        "b_q_a_norm": gain((nB, Q_LORA)),
        "b_w_uq": nrm((nB, Q_LORA, MLA_HEADS * (MLA_NOPE + MLA_ROPE)), Q_LORA ** -0.5),
        "b_w_o": nrm((nB, MLA_HEADS * MLA_V, D_MODEL), (MLA_HEADS * MLA_V) ** -0.5),
        "ffn_norm": gain((DEPTH, D_MODEL)),
        "ffn_w_in": nrm((DEPTH, D_MODEL, 2 * D_FF), D_MODEL ** -0.5),
        "ffn_conv_w": nrm((DEPTH, CONV_W, D_FF), CONV_W ** -0.5),
        "ffn_conv_b": nrm((DEPTH, D_FF), 0.01),
        "ffn_w_out": nrm((DEPTH, D_FF, D_MODEL), D_FF ** -0.5),
        "final_norm": gain((D_MODEL,)),
    }

def first_block(x, meta_tokens, a_attn_norm, a_w_qkv, a_lambda_q1, a_lambda_k1, a_lambda_q2,
              a_lambda_k2, a_sub_norm, a_w_o, kv_norm, kv_w_dkv, kv_a_norm, kv_w_ukv,
              b_attn_norm, b_w_dq, b_q_a_norm, b_w_uq, b_w_o, ffn_norm, ffn_w_in,
              ffn_conv_w, ffn_conv_b, ffn_w_out, final_norm):
    B = x.shape[0]
    meta = jnp.broadcast_to(meta_tokens[None].astype(x.dtype), (B, N_META, D_MODEL))
    h = jnp.concatenate([meta, x], axis=1)
    L = h.shape[1]
    pos = jnp.arange(L, dtype=jnp.int32)
    n_blocks = -(-L // Q_BLOCK)
    kc = chunk_ids(pos)
    qcb = chunk_ids(jnp.arange(n_blocks * Q_BLOCK, dtype=jnp.int32)).reshape(n_blocks, Q_BLOCK)

    k_nope = k_rope = v_shared = None
    for layer in range(DEPTH):
        if layer < N_A_LAYERS:
            h = diff_attn_layer(h, a_attn_norm[layer], a_w_qkv[layer], a_lambda_q1[layer],
                                a_lambda_k1[layer], a_lambda_q2[layer], a_lambda_k2[layer],
                                a_sub_norm[layer], a_w_o[layer], layer, pos, qcb, kc)
        else:
            if layer == N_A_LAYERS:
                k_nope, k_rope, v_shared = shared_latent_kv(h, kv_norm, kv_w_dkv, kv_a_norm,
                                                            kv_w_ukv, pos)
            i = layer - N_A_LAYERS
            h = mla_layer(h, b_attn_norm[i], b_w_dq[i], b_q_a_norm[i], b_w_uq[i], b_w_o[i],
                          k_nope, k_rope, v_shared, pos, qcb, kc)
        h = conv_ffn(h, ffn_norm[layer], ffn_w_in[layer], ffn_conv_w[layer],
                     ffn_conv_b[layer], ffn_w_out[layer])
    return rms_norm(h, final_norm)[:, N_META:]


DEPTH_2 = 1

CONV_WIDTH = D_MODEL
CONV_K = 3
HEAD_DIM = 64
N_Q_HEADS = 8
N_KV_HEADS = 2
GQA_GROUP = N_Q_HEADS // N_KV_HEADS
WINDOW = 128
BLOCK = WINDOW
ROPE_THETA_2 = 10000.0
Q_WIDTH = N_Q_HEADS * HEAD_DIM
KV_WIDTH = N_KV_HEADS * HEAD_DIM
D_FF_2 = 2816
FFN_CONV_K = 3

IN_SIZES = (CONV_WIDTH, CONV_WIDTH, CONV_WIDTH, Q_WIDTH, KV_WIDTH, KV_WIDTH, D_MODEL, D_MODEL)
IN_WIDTH = sum(IN_SIZES)
IN_SPLITS = tuple(int(c) for c in np.cumsum(IN_SIZES)[:-1])


def rmsnorm(x, w):
    xf = x.astype(jnp.float32)
    xf = xf * lax.rsqrt(jnp.mean(xf * xf, axis=-1, keepdims=True) + EPS)
    return xf.astype(x.dtype) * w

def causal_dwconv(v, w, b=None):
    k_taps = w.shape[0]
    s = v.shape[1]
    vp = jnp.pad(v, ((0, 0), (k_taps - 1, 0), (0, 0)))
    y = sum(w[i] * vp[:, i:i + s] for i in range(k_taps))
    if b is not None:
        y = y + b
    return y

def rope_tables(positions, dtype):
    inv_freq = ROPE_THETA_2 ** (-jnp.arange(0, HEAD_DIM, 2, dtype=jnp.float32) / HEAD_DIM)
    ang = positions.astype(jnp.float32)[..., None] * inv_freq
    return jnp.cos(ang)[:, :, None, :].astype(dtype), jnp.sin(ang)[:, :, None, :].astype(dtype)

def apply_rope(x, cos, sin):
    x1, x2 = jnp.split(x, 2, axis=-1)
    return jnp.concatenate([x1 * cos - x2 * sin, x2 * cos + x1 * sin], axis=-1)

def sliding_window_attention(q, k, v, sinks):
    b, s = q.shape[:2]
    nb = s // BLOCK
    qb = q.reshape(b, nb, BLOCK, N_KV_HEADS, GQA_GROUP, HEAD_DIM)

    def with_prev(t):
        tb = t.reshape(b, nb, BLOCK, N_KV_HEADS, HEAD_DIM)
        prev = jnp.pad(tb[:, :-1], ((0, 0), (1, 0), (0, 0), (0, 0), (0, 0)))
        return jnp.concatenate([prev, tb], axis=2)

    kk, vv = with_prev(k), with_prev(v)
    scale = HEAD_DIM ** -0.5
    scores = jnp.einsum('bnqhgd,bnkhd->bnhgqk', qb, kk).astype(jnp.float32) * scale

    q_pos = jnp.arange(BLOCK)[:, None] + BLOCK
    k_pos = jnp.arange(2 * BLOCK)[None, :]
    rel = q_pos - k_pos
    band = (rel >= 0) & (rel < WINDOW)
    not_pad = (jnp.arange(nb)[:, None, None] > 0) | (k_pos[None] >= BLOCK)
    valid = band[None] & not_pad
    scores = jnp.where(valid[None, :, None, None], scores, -jnp.inf)

    sink = sinks.astype(jnp.float32).reshape(N_KV_HEADS, GQA_GROUP)[None, None, :, :, None, None]
    m = jnp.maximum(jnp.max(scores, axis=-1, keepdims=True), sink)
    p = jnp.exp(scores - m)
    denom = jnp.sum(p, axis=-1, keepdims=True) + jnp.exp(sink - m)
    probs = (p / denom).astype(v.dtype)
    out = jnp.einsum('bnhgqk,bnkhd->bnqhgd', probs, vv)
    return out.reshape(b, s, Q_WIDTH)

def second_inputs(seed: int = 0) -> dict:
    key = jax.random.key(seed)
    ks = jax.random.split(key, 20)
    f32 = jnp.float32

    def nrm(k, shape, scale):
        return jax.random.normal(k, shape, f32) * scale

    x = jax.random.normal(ks[0], (BATCH, SEQ, D_MODEL), f32)
    positions = jnp.broadcast_to(jnp.arange(SEQ, dtype=jnp.int32), (BATCH, SEQ))
    return {
        "x": x,
        "positions": positions,
        "norm_mix_w": 1.0 + nrm(ks[1], (DEPTH_2, D_MODEL), 0.02),
        "w_in": nrm(ks[2], (DEPTH_2, D_MODEL, IN_WIDTH), D_MODEL ** -0.5),
        "b_in": nrm(ks[3], (DEPTH_2, IN_WIDTH), 0.02),
        "conv_mix_w": nrm(ks[4], (DEPTH_2, CONV_K, CONV_WIDTH), CONV_K ** -0.5),
        "w_conv_out": nrm(ks[5], (DEPTH_2, CONV_WIDTH, D_MODEL), CONV_WIDTH ** -0.5),
        "w_attn_out": nrm(ks[6], (DEPTH_2, Q_WIDTH, D_MODEL), Q_WIDTH ** -0.5),
        "b_attn_out": nrm(ks[7], (DEPTH_2, D_MODEL), 0.02),
        "sinks": nrm(ks[8], (DEPTH_2, N_Q_HEADS), 1.0),
        "w_mix_out": nrm(ks[9], (DEPTH_2, D_MODEL, D_MODEL), D_MODEL ** -0.5),
        "norm_ffn_w": 1.0 + nrm(ks[10], (DEPTH_2, D_MODEL), 0.02),
        "w_ffn_up": nrm(ks[11], (DEPTH_2, D_MODEL, 2 * D_FF_2), D_MODEL ** -0.5),
        "ffn_conv_w": nrm(ks[12], (DEPTH_2, FFN_CONV_K, D_FF_2), FFN_CONV_K ** -0.5),
        "ffn_conv_b": nrm(ks[13], (DEPTH_2, D_FF_2), 0.02),
        "w_ffn_down": nrm(ks[14], (DEPTH_2, D_FF_2, D_MODEL), D_FF_2 ** -0.5),
        "norm_final_w": 1.0 + nrm(ks[15], (D_MODEL,), 0.02),
    }

def second_block(x, positions, norm_mix_w, w_in, b_in, conv_mix_w, w_conv_out, w_attn_out,
              b_attn_out, sinks, w_mix_out, norm_ffn_w, w_ffn_up, ffn_conv_w, ffn_conv_b,
              w_ffn_down, norm_final_w):
    b, s, _ = x.shape
    cos, sin = rope_tables(positions, x.dtype)
    for l in range(DEPTH_2):
        u = rmsnorm(x, norm_mix_w[l])
        proj = u @ w_in[l] + b_in[l]
        cb, cc, cx, q, k, v, g_conv, g_attn = jnp.split(proj, IN_SPLITS, axis=-1)

        y_conv = (cb * causal_dwconv(cc * cx, conv_mix_w[l])) @ w_conv_out[l]

        q = apply_rope(q.reshape(b, s, N_Q_HEADS, HEAD_DIM), cos, sin)
        k = apply_rope(k.reshape(b, s, N_KV_HEADS, HEAD_DIM), cos, sin)
        v = v.reshape(b, s, N_KV_HEADS, HEAD_DIM)
        y_attn = sliding_window_attention(q, k, v, sinks[l]) @ w_attn_out[l] + b_attn_out[l]

        merged = jax.nn.sigmoid(g_conv) * y_conv + jax.nn.sigmoid(g_attn) * y_attn
        x = x + merged @ w_mix_out[l]

        u = rmsnorm(x, norm_ffn_w[l])
        up, gate = jnp.split(u @ w_ffn_up[l], 2, axis=-1)
        a = causal_dwconv(up, ffn_conv_w[l], ffn_conv_b[l])
        x = x + (jax.nn.silu(a) * gate) @ w_ffn_down[l]
    return rmsnorm(x, norm_final_w)


def setup_inputs(seed=0):
    out = dict(first_inputs(seed))
    for name, value in second_inputs(seed + 1).items():
        if name != "x":
            out[name + "_2"] = value
    return out


def reference(
    x, meta_tokens, a_attn_norm, a_w_qkv, a_lambda_q1, a_lambda_k1, a_lambda_q2, a_lambda_k2,
    a_sub_norm, a_w_o, kv_norm, kv_w_dkv, kv_a_norm, kv_w_ukv, b_attn_norm, b_w_dq, b_q_a_norm,
    b_w_uq, b_w_o, ffn_norm, ffn_w_in, ffn_conv_w, ffn_conv_b, ffn_w_out, final_norm,
    positions_2, norm_mix_w_2, w_in_2, b_in_2, conv_mix_w_2, w_conv_out_2, w_attn_out_2,
    b_attn_out_2, sinks_2, w_mix_out_2, norm_ffn_w_2, w_ffn_up_2, ffn_conv_w_2, ffn_conv_b_2,
    w_ffn_down_2, norm_final_w_2,
):
    x = first_block(
        x, meta_tokens, a_attn_norm, a_w_qkv, a_lambda_q1, a_lambda_k1, a_lambda_q2,
        a_lambda_k2, a_sub_norm, a_w_o, kv_norm, kv_w_dkv, kv_a_norm, kv_w_ukv, b_attn_norm,
        b_w_dq, b_q_a_norm, b_w_uq, b_w_o, ffn_norm, ffn_w_in, ffn_conv_w, ffn_conv_b,
        ffn_w_out, final_norm,
    )
    return second_block(
        x, positions_2, norm_mix_w_2, w_in_2, b_in_2, conv_mix_w_2, w_conv_out_2, w_attn_out_2,
        b_attn_out_2, sinks_2, w_mix_out_2, norm_ffn_w_2, w_ffn_up_2, ffn_conv_w_2,
        ffn_conv_b_2, w_ffn_down_2, norm_final_w_2,
    )


_drawn_inputs = setup_inputs


def setup_inputs(seed=0):
    import zlib

    import numpy as np

    out = dict(_drawn_inputs(seed))
    spreads = {}
    factors = {'kv_norm': 8.0,
     'kv_a_norm': 8.0,
     'b_attn_norm': 8.0,
     'b_q_a_norm': 8.0,
     'ffn_conv_b': 7.058,
     'norm_mix_w_2': 2.924,
     'b_attn_out_2': 44.136,
     'sinks_2': 43.346,
     'norm_ffn_w_2': 13.546,
     'ffn_conv_b_2': 18.775,
     'norm_final_w_2': 8.3,
     'b_in_2': 3.637}
    for name, (base, spread) in spreads.items():
        noise = np.random.default_rng([zlib.crc32(name.encode()), seed]).standard_normal(out[name].shape)
        drawn = base * np.exp(spread * noise) if base else spread * noise
        out[name] = __import__('jax').numpy.asarray(drawn.astype(out[name].dtype))
    for name, factor in factors.items():
        out[name] = (out[name] * factor).astype(out[name].dtype)
    return out
```

```python
from contextlib import ExitStack

import numpy as np

import concourse.bass as bass
from concourse import mybir

F32 = mybir.dt.float32
F32R = mybir.dt.float32r
I32 = mybir.dt.int32
ALU = mybir.AluOpType
ACT = mybir.ActivationFunctionType
AX = mybir.AxisListType

P = 128
D = 1024
KD = D // P
META = 16
SEQ = 512
T1 = META + SEQ
T2 = SEQ
CH = T1 // 2
HEADS_A = 8
HEADS_B = 16
NOPE, ROPE = 64, 32
QB = 96
KKV = 2
KQ = 3
FF = 2816 // P
GROUPS = (8, 8, 6)
HB = 8
HW = HB * P
EPS = 1e-5
LAM_INIT = 0.8 - 0.6
NEG = -1.0e30
TILES_C = 47

J_A = 0
J_WO = J_A + 4 * HEADS_A
J_F0 = J_WO + KD
FFN_HALVES = sum(2 * g + KD for g in GROUPS)
J_DD = J_F0 + FFN_HALVES
J_B = J_DD + 6
J_BO = J_B + HEADS_B
J_F1 = J_BO + KD
J_C = J_F1 + FFN_HALVES
J_CO = J_C + TILES_C
J_AO = J_CO + KD
J_MX = J_AO + KD
J_F2 = J_MX + KD
HALVES = J_F2 + FFN_HALVES

TL_WO = 0
TL_F0 = TL_WO + KD
TL_DD = TL_F0 + FFN_HALVES
TL_BO = TL_DD + 6
TL_F1 = TL_BO + KD
TL_C = TL_F1 + FFN_HALVES
TL_CO = TL_C + TILES_C
TL_AO = TL_CO + KD
TL_MX = TL_AO + KD
TL_F2 = TL_MX + KD

PAR_SIZES = (("a_attn_norm", 8), ("ffn_norm0", 8), ("kv_norm", 8), ("b_attn_norm", 8), ("ffn_norm1", 8),
             ("final_norm", 8), ("norm_mix", 8), ("norm_ffn2", 8), ("final_norm2", 8), ("a_sub", 1),
             ("kv_a", KKV), ("q_a", KQ), ("conv0", 3 * FF), ("convb0", FF), ("conv1", 3 * FF), ("convb1", FF),
             ("conv2", 3 * FF), ("convb2", FF), ("conv_mix", 3 * KD), ("b_in", TILES_C), ("b_attn_out", 8),
             ("sinks", 8), ("lam", 4 * 64))
PAR, NPAR = {}, 0
for _name, _n in PAR_SIZES:
    PAR[_name] = NPAR
    NPAR += _n

N_A, N_SUB, N_F0, N_DD, N_KV, N_KQ, N_BO, N_FIN1, N_MIX, N_F2, N_FIN2 = 0, 1, 9, 10, 11, 12, 13, 14, 15, 16, 17
ACC = {N_A: 0, N_F0: 9, N_DD: 18, N_KV: 27, N_KQ: 28, N_BO: 30, N_FIN1: 39, N_MIX: 48, N_F2: 57, N_FIN2: 66}
SQ = {N_A: 0, N_SUB: 8, N_F0: 16, N_DD: 24, N_KV: 32, N_KQ: 34, N_BO: 37, N_FIN1: 45, N_MIX: 53, N_F2: 61, N_FIN2: 69}
X_A, X_F0, X_KV, X_CKV, X_CQ, X_F1, X_C, X_AO, X_F2 = 0, 8, 16, 24, 26, 29, 37, 45, 49
G_WO, G_F0, G_DQ, G_BO, G_F1, G_CO, G_MX, G_F2 = 0, 8, 30, 38, 46, 68, 76, 84

SWAP8 = [i + 8 if i < 8 else i - 8 if i < 16 else i for i in range(32)]
SWAP16 = [(i + 16) % 32 for i in range(32)]

TWO_PI_A = 6.28125
TWO_PI_B = 0.0019350051879882812
TWO_PI_C = float(2 * np.pi - TWO_PI_A - TWO_PI_B)
ROUND = 12582912.0


def rotary_tables():
    pos = np.arange(T1, dtype=np.float32)
    tabs = np.zeros((4, P, T1), np.float32)
    tabs[0], tabs[2] = 1.0, 1.0
    inv = (1.0 / (np.float32(500000.0) ** (np.arange(8, dtype=np.float32) / 8))).astype(np.float32)
    for block in (0, 64):
        for i in range(8):
            ang = pos * inv[i]
            for row, sign in ((block + i, -1.0), (block + 8 + i, 1.0)):
                tabs[0, row], tabs[1, row] = np.cos(ang), sign * np.sin(ang)
    inv = (1.0 / (np.float32(10000.0) ** (np.arange(16, dtype=np.float32) / 16))).astype(np.float32)
    for i in range(16):
        ang = pos * inv[i]
        for row, sign in ((NOPE + i, -1.0), (NOPE + 16 + i, 1.0)):
            tabs[2, row], tabs[3, row] = np.cos(ang), sign * np.sin(ang)
    tabs[0:2] *= np.float32(64.0 ** -0.25)
    tabs[2:4] *= np.float32(96.0 ** -0.25)
    return tabs


def shape_constants():
    c = np.zeros((P, 3 * P + 2), np.float32)
    c[:, 0:P] = np.eye(P)
    q, k = np.arange(P)[:, None], np.arange(P)[None, :]
    c[:, P:2 * P] = np.where(k > q, 0.0, NEG)
    c[:, 2 * P:3 * P] = np.where(k <= q, 0.0, NEG)
    inv = (np.float32(10000.0) ** (-np.arange(0, 64, 2, dtype=np.float32) / 64)).astype(np.float32)
    for p in range(P):
        n = p % 64
        c[p, 3 * P] = inv[16 * (n // 32) + n % 16]
        c[p, 3 * P + 1] = -1.0 if n % 32 < 16 else 1.0
    return c


def unit2_at(u):
    return 8 + 11 * u // 4


def wait(eng, semaphore, value):
    if not isinstance(value, int) or value > 0:
        eng.wait_ge(semaphore, value)


def program(nc, x_t, stream, params, positions, out):
    tabs_dram = nc.inline_tensor(rotary_tables(), "rotary_tables").ap()
    consts_dram = nc.inline_tensor(shape_constants(), "shape_constants").ap()
    with ExitStack() as ctx:
        def sb(name, shape, dt=F32):
            return ctx.enter_context(nc.sbuf_tensor(name, shape, dt))

        def sem(name):
            return ctx.enter_context(nc.semaphore(name))

        w_raw = sb("w_raw", [P, 4, HW])
        w_hi = sb("w_hi", [P, 4, HW], F32R)
        w_lo = sb("w_lo", [P, 4, HW], F32R)
        h = sb("h", [P, KD, T1])
        x_hi = sb("x_hi", [P, KD, T1], F32R)
        x_lo = sb("x_lo", [P, KD, T1], F32R)
        g_hi = sb("g_hi", [P, KD, T1], F32R)
        g_lo = sb("g_lo", [P, KD, T1], F32R)
        par = sb("par", [P, NPAR])
        cst = sb("cst", [P, 3 * P + 2])
        ones = sb("ones", [P, P])
        small = sb("small", [P, 128])
        acc = sb("acc", [P, T1])
        r = sb("r", [P, T1])
        sq = sb("sq", [P, 2, T1])
        SCRATCH = 14400
        scratch = sb("scratch", [P, SCRATCH])
        ident = cst[:, 0:P]
        at = [0]

        def carve(n):
            at[0] += n
            assert at[0] <= SCRATCH
            return scratch[:, at[0] - n:at[0]]

        k_buf = carve(2 * T1).rearrange("p (a t) -> p a t", a=2)
        q_buf = carve(2 * T1).rearrange("p (a t) -> p a t", a=2)
        vt_buf = carve(T1)
        v_tok = carve(2 * 512).rearrange("p (a n) -> p a n", a=2)
        v_meta = carve(2 * P).rearrange("p (a n) -> p a n", a=2)
        o_buf = carve(KD * T1).rearrange("p (k t) -> p k t", k=KD)
        prob = carve(4 * T1).rearrange("p (a m t) -> p a m t", a=2, m=2)
        pt = carve(2 * 512).rearrange("p (a n) -> p a n", a=2)
        pt_meta = carve(2 * P).rearrange("p (a n) -> p a n", a=2)
        cos_r = carve(T1)
        sin_r = carve(T1)
        cos_t = carve(T1)
        sin_t = carve(T1)
        swapped = carve(T1)
        latent = o_buf
        r_lat = vt_buf
        at[0] = 0
        a_pad = carve(T1 + 2)
        conv = carve(T1)
        silu = carve(T1)
        b_val = carve(T1)
        hid = carve(T1)
        at[0] = 0
        y_val = carve(2 * T2).rearrange("p (a t) -> p a t", a=2)
        cc_val = carve(T2)
        cx_val = carve(T2)
        cb_val = carve(T2)
        mix_pad = carve(T2 + 2)
        mix_conv = carve(T2)
        mix_val = carve(T2)
        o2 = carve(4 * T2).rearrange("p (g t) -> p g t", g=4)
        at_gates = at[0]
        k2 = carve(2 * T2).rearrange("p (g t) -> p g t", g=2)
        q2 = carve(4 * T2).rearrange("p (g t) -> p g t", g=4)
        vt2 = carve(T2)
        v2 = carve(T2).rearrange("p (b n) -> p b n", b=4)
        prob2 = carve(4 * 256).rearrange("p (i k) -> p i k", i=4)
        pt2 = carve(2 * 512).rearrange("p (b n) -> p b n", b=2)
        cos2 = carve(T2)
        sin2 = carve(T2)
        swapped2 = carve(T2)
        at[0] = at_gates
        gates = carve(2 * KD * T2).rearrange("p (g t) -> p g t", g=2 * KD)
        ang = prob2[:, :, :].rearrange("p i k -> p (i k)")[:, 0:T2]
        turns = prob2[:, :, :].rearrange("p i k -> p (i k)")[:, T2:2 * T2]
        red = pt2[:, 0, :]
        pos_f = pt2[:, 1, :]
        pos_i = turns.bitcast(I32)
        neg_max = small[:, 0:8]
        sums = small[:, 8:16]
        recips = small[:, 16:24]
        neg_lam = small[:, 24:25]
        lam_dot = small[:, 26:28]
        lam_exp = small[:, 28:30]
        sub_gain = small[:, 32:33]
        eps = small[:, 33:34]
        max2 = small[:, 40:44]
        neg2 = small[:, 44:48]
        sink_arg = small[:, 48:52]
        sink_exp = small[:, 52:56]
        sum2 = small[:, 56:60]
        den2 = small[:, 60:64]
        rec2 = small[:, 64:68]
        ps = ctx.enter_context(nc.psum_tensor("ps", [P, 8, 512], F32))
        flat = ps[:, :, :].rearrange("p b c -> p (b c)")

        x_loaded = [sem(f"x_loaded{i}") for i in range(4)]
        par_loaded = sem("par_loaded")
        cst_loaded = sem("cst_loaded")
        tab_loaded = sem("tab_loaded")
        tab2_loaded = sem("tab2_loaded")
        pos_loaded = sem("pos_loaded")
        raw_loaded = [sem(f"raw_loaded{i}") for i in range(4)]
        hi_ready = sem("hi_ready")
        lo_ready = sem("lo_ready")
        half_done = sem("half_done")
        chunk_done = sem("chunk_done")
        chunk_taken = sem("chunk_taken")
        kv_taken = sem("kv_taken")
        tile_taken = sem("tile_taken")
        sq_ready = sem("sq_ready")
        acc_step = sem("acc_step")
        ss_ready = sem("ss_ready")
        ln_done = sem("ln_done")
        r_ready = sem("r_ready")
        xh_done = sem("xh_done")
        x_ready = sem("x_ready")
        gh_done = sem("gh_done")
        g_ready = sem("g_ready")
        consts_set = sem("consts_set")
        lam_step = sem("lam_step")
        lam_exp_done = sem("lam_exp_done")
        tabs_made = sem("tabs_made")
        rot_step = sem("rot_step")
        qk_ready = sem("qk_ready")
        vt_done = sem("vt_done")
        v_ready = sem("v_ready")
        s_done = sem("s_done")
        corner_set = sem("corner_set")
        max_done = sem("max_done")
        exp_done = sem("exp_done")
        comb_step = sem("comb_step")
        a_ready = sem("a_ready")
        t_done = sem("t_done")
        pt_ready = sem("pt_ready")
        pv_done = sem("pv_done")
        o_taken = sem("o_taken")
        sub_step = sem("sub_step")
        krope_step = sem("krope_step")
        lat_step = sem("lat_step")
        conv_start = sem("conv_start")
        conv_step = sem("conv_step")
        silu_ready = sem("silu_ready")
        hid_step = sem("hid_step")
        pads_set = sem("pads_set")
        ang_step = sem("ang_step")
        tab2_made = sem("tab2_made")
        y_ready = sem("y_ready")
        rot2_step = sem("rot2_step")
        k2q2_ready = sem("k2q2_ready")
        vt2_done = sem("vt2_done")
        v2_ready = sem("v2_ready")
        s2_done = sem("s2_done")
        masked = sem("masked")
        max2_step = sem("max2_step")
        exp2_done = sem("exp2_done")
        sink_done = sem("sink_done")
        den_step = sem("den_step")
        p2_ready = sem("p2_ready")
        t2_done = sem("t2_done")
        pt2_ready = sem("pt2_ready")
        pv2_done = sem("pv2_done")
        o2_taken = sem("o2_taken")
        mix_step = sem("mix_step")
        mix_start = sem("mix_start")
        merge_step = sem("merge_step")
        h2_ready = sem("h2_ready")
        fin_ready = sem("fin_ready")
        stored = sem("stored")

        def chunks(T):
            return [(0, 0, CH), (1, CH, CH)] if T == T1 else [(0, 0, T2)]

        def result(j, T):
            b = 2 * (j % 2)
            return ps[:, b:b + 2, 0:CH] if T == T1 else ps[:, b, 0:T2]

        def cut(ap, T):
            return ap.rearrange("p (c n) -> p c n", c=2) if T == T1 else ap

        def tok(T):
            return slice(0, T1) if T == T1 else slice(META, T1)

        def pcol(name, i=0):
            return par[:, PAR[name] + i:PAR[name] + i + 1]

        UNITS = 5

        def unit(idx):
            t = 4 - idx
            nq = P if t else META
            return t, nq, (META + P * (t - 1) if t else 0)

        def s_base(kind, idx, m):
            return (2 + 2 * (m if kind == "A" else idx % 2)) * 512 + 512 - META

        block = ctx.enter_context(nc.Block())

        @block.sync
        def _(sp):
            for i in range(4):
                sp.dma_start(h[:, 2 * i:2 * i + 2, :], x_t[:, 2 * i:2 * i + 2, :]).then_inc(x_loaded[i], 16)

            def load_half(j, i=0):
                wait(sp, lo_ready, j - 3 + 4 * i)
                sp.dma_start(w_raw[:, j % 4, :], stream[j + 4 * i]).then_inc(raw_loaded[j % 4], 16)

            for j in range(4):
                load_half(j)
            with sp.Fori(0, HALVES // 4 - 1) as i:
                for j in range(4, 8):
                    load_half(j, i)
            for j in range(HALVES // 4 * 4, HALVES):
                load_half(j)
            for m in range(KD):
                sp.wait_ge(fin_ready, m + 1)
                sp.dma_start(out[:, m, :], h[:, m, META:T1]).then_inc(stored, 16)
            sp.wait_ge(stored, 16 * KD)

        @block.gpsimd
        def _(pool):
            def lo_part(j, i=0):
                pool.wait_ge(hi_ready, j + 1 + 4 * i)
                wait(pool, half_done, j - 3 + 4 * i)
                nc.gpsimd.tensor_tensor(w_lo[:, j % 4, :], w_raw[:, j % 4, :], w_hi[:, j % 4, :].bitcast(F32),
                                        ALU.subtract).then_inc(lo_ready, 1)

            for j in range(4):
                lo_part(j)
            with pool.Fori(0, HALVES // 4 - 1) as i:
                for j in range(4, 8):
                    lo_part(j, i)
            for j in range(HALVES // 4 * 4, HALVES):
                lo_part(j)

        @block.tensor
        def _(pe):
            def passes(out_ap, j, b, xh, xl, k, cols, first, last):
                s, c = j % 4, slice(b * P, (b + 1) * P)
                nc.tensor.matmul(out_ap, w_hi[:, s, c], xh[:, k, cols], start=first, stop=False)
                nc.tensor.matmul(out_ap, w_hi[:, s, c], xl[:, k, cols], start=False, stop=False)
                return nc.tensor.matmul(out_ap, w_lo[:, s, c], xh[:, k, cols], start=False, stop=last)

            def tile(j, tl, blocks, xh, xl, T, ready, i=0):
                pe.wait_ge(lo_ready, j + 1 + 4 * i)
                wait(pe, tile_taken, tl - 1 + 4 * i)
                for bank, t0, n in chunks(T):
                    for b in range(blocks):
                        if ready and not bank:
                            pe.wait_ge(ready[0], ready[1] + b + 1)
                        last = passes(ps[:, 2 * (j % 2) + bank, 0:n], j, b, xh, xl, b, slice(t0, t0 + n),
                                      b == 0, b == blocks - 1)
                last.then_inc(half_done, 1)

            def tiles(j, tl, n, blocks, xh, xl, T, ready, after_first=None):
                done = 0
                if after_first:
                    tile(j, tl, blocks, xh, xl, T, ready)
                    after_first()
                    done = 1
                turns = (n - done) // 4
                if turns > 1 and tl > 1:
                    with pe.Fori(0, turns) as i:
                        for m in range(4):
                            tile(j + done + m, tl + done + m, blocks, xh, xl, T, ready, i)
                    done += 4 * turns
                for m in range(done, n):
                    tile(j + m, tl + m, blocks, xh, xl, T, ready)

            def norm_sum(steps, T, src=acc, semaphore=acc_step, bank0=6):
                pe.wait_ge(semaphore, steps)
                for bank, t0, n in chunks(T):
                    last = nc.tensor.matmul(ps[:, bank0 + bank, 0:n], ones[:, :], src[:, t0:t0 + n],
                                            start=True, stop=True)
                last.then_inc(ss_ready, 1)

            def ffn(j, tl, x0, g0, T, norm):
                for n, g in enumerate(GROUPS):
                    tiles(j, tl, 2 * g, KD, x_hi, x_lo, T, (x_ready, x0),
                          None if n else lambda: norm_sum(ACC[norm] + 9, T))
                    j, tl = j + 2 * g, tl + 2 * g
                    tiles(j, tl, KD, g, g_hi, g_lo, T, (g_ready, g0))
                    j, tl, g0 = j + KD, tl + KD, g0 + g

            def small_next():
                pe.wait_ge(cst_loaded, 16)

            def piece_a(hd, p):
                m, c = divmod(p, 2)
                wait(pe, chunk_taken, 6 * hd + p - 1)
                for k in range(KD):
                    b = KD * m + k
                    if not c and (k == 0 or b % 6 == 0):
                        pe.wait_ge(lo_ready, J_A + 4 * hd + b // 6 + 1)
                    if isinstance(hd, int) and hd == 0 and p == 0:
                        pe.wait_ge(x_ready, X_A + k + 1)
                    last = passes(ps[:, c, 0:CH], J_A + b // 6, b % 6, x_hi, x_lo, k,
                                  slice(c * CH, c * CH + CH), k == 0, k == KD - 1)
                    if c and (b % 6 == 5):
                        last.then_inc(half_done, 1)
                if p < 5:
                    last.then_inc(chunk_done, 1)

            def piece_b(hd, s, p):
                m, c = divmod(p, 2)
                if m == 0:
                    wait(pe, chunk_taken, 6 * HEADS_A + 2 * hd + c - 1 if not isinstance(hd, int) or hd else 0)
                else:
                    pe.wait_ge(kv_taken, 2 * hd + c + 1)
                if p == 0:
                    pe.wait_ge(lo_ready, J_B + hd + 1)
                if isinstance(hd, int) and hd == 0 and not c:
                    pe.wait_ge(x_ready, X_CKV + (KKV + KQ if m else KKV))
                n, k0 = (KQ, KKV) if m else (KKV, 0)
                for k in range(n):
                    last = passes(ps[:, c, 0:CH], J_B + s, k0 + k, x_hi, x_lo, k0 + k,
                                  slice(c * CH, c * CH + CH), k == 0, k == n - 1)
                last.then_inc(half_done if p == 3 else chunk_done, 1)

            def scores(kind, hd, par_, idx):
                t, nq, q0 = unit(idx)
                u = (5 * hd if kind == "A" else 5 * HEADS_A + 5 * hd) + idx
                if idx == 0:
                    pe.wait_ge(qk_ready, 2 * hd + 2 if kind == "A" else 2 * HEADS_A + hd + 1)
                    if kind == "B":
                        pe.wait_ge(kv_taken, 2 * hd + 2)
                        if isinstance(hd, int) and hd == 0:
                            pe.wait_ge(krope_step, 2)
                if kind == "A" and not t:
                    small_next()
                if kind == "A":
                    wait(pe, exp_done, u)
                else:
                    wait(pe, exp_done, u - 1 if idx else u)
                for m in range(2 if kind == "A" else 1):
                    rows = slice(64 * m, 64 * m + 64) if kind == "A" else slice(0, QB)
                    b = s_base(kind, idx, m)
                    q = q_buf[rows, par_, q0:q0 + nq]
                    last = nc.tensor.matmul(flat[0:nq, b:b + META], q, k_buf[rows, par_, 0:META],
                                            start=True, stop=True)
                    if t:
                        last = nc.tensor.matmul(flat[0:nq, b + META:b + META + P * t], q,
                                                k_buf[rows, par_, META:META + P * t], start=True, stop=True)
                last.then_inc(s_done, 1)

            def transposes(kind, hd, par_, idx):
                t, nq, _ = unit(idx)
                u = (5 * hd if kind == "A" else 5 * HEADS_A + 5 * hd) + idx
                up = (par_ + idx) % 2
                pe.wait_ge(a_ready, u + 1)
                wait(pe, pt_ready, u)
                if idx == 0:
                    pe.wait_ge(v_ready, (hd if kind == "A" else HEADS_A + hd) + 1)
                    wait(pe, o_taken, u)
                for b in range(t):
                    last = nc.tensor.transpose(ps[:, 6, b * P:b * P + nq],
                                               prob[0:nq, up, 0, META + b * P:META + b * P + P], ident[0:nq, 0:nq])
                bank, c = (7, 0) if t == 4 else (6, t * P)
                last = nc.tensor.transpose(ps[0:META, bank, c:c + P], prob[:, up, 0, 0:META], ident)
                last.then_inc(t_done, 1)

            def values(kind, hd, par_, idx):
                t, nq, _ = unit(idx)
                u = (5 * hd if kind == "A" else 5 * HEADS_A + 5 * hd) + idx
                up = (par_ + idx) % 2
                pe.wait_ge(pt_ready, u + 1)
                wait(pe, o_taken, u)
                w = P if kind == "A" else 64
                rows = slice(0, P) if kind == "A" else slice(64 * par_, 64 * par_ + 64)
                o = ps[rows, 7, P:P + nq]
                for b in range(t):
                    nc.tensor.matmul(o, v_tok[:, par_, b * w:b * w + w], pt[:, up, b * P:b * P + nq],
                                     start=b == 0, stop=False)
                nc.tensor.matmul(o, v_meta[0:META, par_, 0:w], pt_meta[0:META, up, 0:nq],
                                 start=t == 0, stop=True).then_inc(pv_done, 1)

            def value_transposes(kind, hd, par_):
                u = 5 * hd if kind == "A" else 5 * HEADS_A + 5 * hd
                pe.wait_ge(*((chunk_taken, 6 * hd + 6) if kind == "A" else (kv_taken, 2 * hd + 2)))
                wait(pe, pt_ready, u)
                wait(pe, o_taken, u)
                for b in range(4):
                    nc.tensor.transpose(ps[:, 6, b * P:b * P + P], vt_buf[:, META + b * P:META + b * P + P], ident)
                nc.tensor.transpose(ps[0:META, 7, 0:P], vt_buf[:, 0:META], ident).then_inc(vt_done, 1)

            def head_a(hd, par_, more=True):
                def step(f, idx):
                    f("A", hd, par_, idx)

                def piece(p):
                    if more:
                        piece_a(hd + 1, p)
                value_transposes("A", hd, par_)
                piece(0)
                step(transposes, 0), step(scores, 1)
                piece(1)
                step(values, 0), step(transposes, 1), step(scores, 2)
                piece(2)
                step(values, 1), step(transposes, 2), step(scores, 3)
                piece(3)
                step(values, 2), step(transposes, 3), step(scores, 4)
                piece(4)
                step(values, 3), step(transposes, 4)
                if more:
                    scores("A", hd + 1, 1 - par_, 0)
                piece(5)
                step(values, 4)

            def head_b(hd, par_, s, more=True):
                def step(f, idx):
                    f("B", hd, par_, idx)

                def piece(p):
                    if more:
                        piece_b(hd + 1, s + 1, p)
                value_transposes("B", hd, par_)
                piece(0)
                step(transposes, 0), step(scores, 2)
                piece(1)
                step(values, 0), step(transposes, 1), step(scores, 3)
                piece(2)
                step(values, 1), step(transposes, 2), step(scores, 4)
                piece(3)
                step(values, 2), step(transposes, 3), step(values, 3)
                step(transposes, 4)
                if more:
                    scores("B", hd + 1, 1 - par_, 0)
                    scores("B", hd + 1, 1 - par_, 1)
                step(values, 4)

            pe.wait_ge(consts_set, 1)
            pe.wait_ge(cst_loaded, 16)
            for p in range(6):
                piece_a(0, p)
                if p == 0:
                    norm_sum(ACC[N_A] + 9, T1)
            scores("A", 0, 0, 0)
            head_a(0, 0)
            with pe.Fori(0, (HEADS_A - 2) // 2) as i:
                for n in range(2):
                    head_a(2 * i + 1 + n, (1 + n) % 2)
            head_a(HEADS_A - 1, 1, more=False)
            pe.wait_ge(o_taken, 5 * HEADS_A)
            for n in range(HEADS_A):
                if n >= 2:
                    pe.wait_ge(r_ready, N_SUB + n - 1)
                norm_sum(SQ[N_SUB] + n + 1, T1, sq[:, n % 2, :], sq_ready, 4 + 2 * (n % 2))
            tiles(J_WO, TL_WO, KD, KD, g_hi, g_lo, T1, (g_ready, G_WO))
            ffn(J_F0, TL_F0, X_F0, G_F0, T1, N_F0)
            for m in range(6):
                xh, xl, ready = (x_hi, x_lo, (x_ready, X_KV)) if m < 3 else (g_hi, g_lo, (g_ready, G_DQ))
                tile(J_DD + m, TL_DD + m, KD, xh, xl, T1, ready)
                if m == 0:
                    norm_sum(ACC[N_DD] + 9, T1)
                if m == 3:
                    norm_sum(ACC[N_KV] + 1, T1)
            norm_sum(ACC[N_KQ] + 2, T1)
            pe.wait_ge(tile_taken, TL_BO)
            for p in range(4):
                piece_b(0, 0, p)
            scores("B", 0, 0, 0)
            scores("B", 0, 0, 1)
            head_b(0, 0, 0)
            with pe.Fori(0, 3) as i:
                for n in range(4):
                    head_b(4 * i + 1 + n, (1 + n) % 2, 1 + n)
            for n in range(13, HEADS_B):
                head_b(n, n % 2, n, more=n < HEADS_B - 1)
            tiles(J_BO, TL_BO, KD, KD, g_hi, g_lo, T1, (g_ready, G_BO))
            ffn(J_F1, TL_F1, X_F1, G_F1, T1, N_BO)

            norm_sum(ACC[N_FIN1] + 9, T2)
            for m in range(TILES_C):
                tile(J_C + m, TL_C + m, KD, x_hi, x_lo, T2, (x_ready, X_C))
                if m == 0:
                    norm_sum(ACC[N_MIX] + 9, T2)
                if m == 4:
                    pe.wait_ge(y_ready, 3)
                    for b in range(4):
                        last = nc.tensor.transpose(ps[:, 3, b * P:b * P + P], vt2[:, b * P:b * P + P], ident)
                    last.then_inc(vt2_done, 1)
                for u in range(8):
                    g, n = divmod(u, 4)
                    s_at = unit2_at(u)
                    k0 = 0 if n else P
                    if m == s_at + 2:
                        pe.wait_ge(p2_ready, u + 1)
                        wait(pe, pt2_ready, u)
                        for i in range(4):
                            for kb in range(k0 // P, 2):
                                last = nc.tensor.transpose(ps[:, 6 + kb, i * P:i * P + P],
                                                           prob2[:, i, kb * P:kb * P + P], ident)
                        last.then_inc(t2_done, 1)
                    if m == s_at + 3:
                        pe.wait_ge(pt2_ready, u + 1)
                        pe.wait_ge(v2_ready, 1)
                        wait(pe, o2_taken, 2 * u)
                        for kb in range(k0 // P, 2):
                            last = nc.tensor.matmul(ps[0:64, 1, :], v2[:, n - 1 + kb, g * 64:g * 64 + 64],
                                                    pt2[:, kb, :], start=kb == k0 // P, stop=kb == 1)
                        last.then_inc(pv2_done, 1)
                for u in range(8):
                    g, n = divmod(u, 4)
                    k0 = 0 if n else P
                    if m == unit2_at(u):
                        pe.wait_ge(k2q2_ready, 6)
                        wait(pe, masked, u)
                        for i in range(4):
                            e, pair = divmod(i, 2)
                            rows = slice(64 * e, 64 * e + 64)
                            last = nc.tensor.matmul(ps[:, 4 + e, pair * 256 + k0:pair * 256 + 256],
                                                    q2[rows, 2 * g + pair, n * P:n * P + P],
                                                    k2[rows, g, (n - 1) * P + k0:(n + 1) * P],
                                                    start=True, stop=True)
                        last.then_inc(s2_done, 1)
            tiles(J_CO, TL_CO, KD, KD, g_hi, g_lo, T2, (g_ready, G_CO))
            tiles(J_AO, TL_AO, KD, 4, x_hi, x_lo, T2, (x_ready, X_AO))
            tiles(J_MX, TL_MX, KD, KD, g_hi, g_lo, T2, (g_ready, G_MX))
            ffn(J_F2, TL_F2, X_F2, G_F2, T2, N_F2)
            norm_sum(ACC[N_FIN2] + 9, T2)

        @block.vector
        def _(dve):
            V = nc.vector

            def square_sum(m, norm, T, i=0):
                dve.wait_ge(sq_ready, SQ[norm] + m + 1 + 4 * i)
                dve.wait_ge(acc_step, ACC[norm] + m + 1 + 4 * i)
                V.tensor_tensor(acc[:, 0:T], acc[:, 0:T], sq[:, m % 2, 0:T], ALU.add).then_inc(acc_step, 1)

            def clear_acc(norm):
                wait(dve, ss_ready, norm)
                V.memset(acc[:, :], 0.0).then_inc(acc_step, 1)

            def scaled_operand(m, gain, x0, T, i=0):
                g = par[:, bass.ds(PAR[gain] + m + 4 * i, 1)] if not isinstance(i, int) else pcol(gain, m)
                hm = h[:, m + 4 * i, tok(T)]
                V.tensor_scalar(x_hi[:, m + 4 * i, 0:T], hm, g, None, ALU.mult).then_inc(xh_done, 1)
                dve.wait_ge(xh_done, x0 + m + 1 + 4 * i)
                V.scalar_tensor_tensor(x_lo[:, m + 4 * i, 0:T], hm, g, x_hi[:, m + 4 * i, 0:T].bitcast(F32),
                                       ALU.mult, ALU.subtract).then_inc(x_ready, 1)

            def parts(src, hi, lo, done, count, ready):
                V.tensor_copy(hi, src).then_inc(done, 1)
                dve.wait_ge(done, count + 1)
                V.tensor_tensor(lo, src, hi.bitcast(F32), ALU.subtract).then_inc(ready, 1)

            def residual(j, tl, T, norm=None, gain=None, x0=0, Tn=None):
                Tn = Tn or T
                if norm is not None:
                    clear_acc(norm)
                with dve.Fori(0, KD // 4) as i:
                    for m in range(4):
                        dve.wait_ge(half_done, j + m + 1 + 4 * i)
                        hm = cut(h[:, m + 4 * i, tok(T)], T)
                        V.tensor_tensor(hm, result(j + m, T), hm, ALU.add).then_inc(tile_taken, 1)
                        if norm is not None:
                            dve.wait_ge(tile_taken, tl + m + 1 + 4 * i)
                            if gain:
                                scaled_operand(m, gain, x0, T, i)
                            square_sum(m, norm, Tn, i)

            def ffn_pair(j, tl, jj, f, layer, g0, T, i=0):
                pair = FF * layer + f

                def tap(k):
                    o = PAR[f"conv{layer}"] + FF * k + f
                    return par[:, o:o + 1] if isinstance(i, int) else par[:, bass.ds(o + 2 * i, 1)]
                dve.wait_ge(half_done, j + 1 + 4 * i)
                V.tensor_tensor(cut(a_pad[:, 2:2 + T], T), result(j, T), cut(r[:, 0:T], T),
                                ALU.mult).then_inc(tile_taken, 1)
                dve.wait_ge(conv_start, pair + 1 + 2 * i)
                dve.wait_ge(tile_taken, tl + 1 + 4 * i)
                V.scalar_tensor_tensor(conv[:, 0:T], a_pad[:, 1:1 + T], tap(1), conv[:, 0:T],
                                       ALU.mult, ALU.add).then_inc(conv_step, 1)
                dve.wait_ge(conv_step, 2 * pair + 1 + 4 * i)
                V.scalar_tensor_tensor(conv[:, 0:T], a_pad[:, 2:2 + T], tap(2), conv[:, 0:T],
                                       ALU.mult, ALU.add).then_inc(conv_step, 1)
                dve.wait_ge(half_done, j + 2 + 4 * i)
                V.tensor_tensor(cut(b_val[:, 0:T], T), result(j + 1, T), cut(r[:, 0:T], T),
                                ALU.mult).then_inc(tile_taken, 1)
                dve.wait_ge(silu_ready, pair + 1 + 2 * i)
                dve.wait_ge(g_ready, g0 + 2 * i)
                dve.wait_ge(tile_taken, tl + 2 + 4 * i)
                V.tensor_tensor(hid[:, 0:T], silu[:, 0:T], b_val[:, 0:T], ALU.mult).then_inc(hid_step, 1)
                dve.wait_ge(hid_step, layer + 1 + pair + 1 + 2 * i)
                parts(hid[:, 0:T], g_hi[:, jj + 2 * i, 0:T], g_lo[:, jj + 2 * i, 0:T],
                      gh_done, g0 + 2 * i, g_ready)

            def ffn(j, tl, layer, g0, T, norm, norm_next, gain=None, x0=0, Tn=None):
                f = 0
                V.memset(a_pad[:, 0:2], 0.0).then_inc(hid_step, 1)
                dve.wait_ge(r_ready, norm + 1)
                for n, g in enumerate(GROUPS):
                    with dve.Fori(0, g // 2) as i:
                        for q in range(2):
                            ffn_pair(j + 2 * q, tl + 2 * q, q, f + q, layer, g0 + q, T, i)
                    j, tl, f, g0 = j + 2 * g, tl + 2 * g, f + g, g0 + g
                    if n < len(GROUPS) - 1:
                        residual(j, tl, T)
                    else:
                        residual(j, tl, T, norm_next, gain, x0, Tn)
                    j, tl = j + KD, tl + KD

            def rotate(rows, dst, steps):
                dve.wait_ge(rot_step, steps + 2)
                V.tensor_tensor(swapped[rows, :], swapped[rows, :], (sin_r if rows.start == 0 else sin_t)[rows, :],
                                ALU.mult).then_inc(rot_step, 1)
                dve.wait_ge(rot_step, steps + 3)
                V.tensor_tensor(dst, dst, swapped[rows, :], ALU.add).then_inc(qk_ready, 1)

            def piece_a(hd, par_, p):
                m, c = divmod(p, 2)
                cols = slice(c * CH, c * CH + CH)
                if p < 5:
                    dve.wait_ge(chunk_done, 5 * hd + p + 1)
                else:
                    dve.wait_ge(half_done, J_A + 4 * hd + 4)
                src = ps[:, c, 0:CH]
                if m == 2:
                    V.tensor_tensor(vt_buf[:, cols], src, r[:, cols], ALU.mult).then_inc(chunk_taken, 1)
                    return
                dst = (k_buf, q_buf)[m]
                if not c:
                    wait(dve, qk_ready, 2 * hd + m)
                V.tensor_tensor(dst[:, par_, cols], src, cos_r[:, cols], ALU.mult).then_inc(rot_step, 1)
                V.stream_shuffle(swapped[:, cols], src, SWAP8).then_inc(chunk_taken, 1)
                if c:
                    dve.wait_ge(chunk_taken, 6 * hd + p + 1)
                    rotate(slice(0, P), dst[:, par_, :], 6 * hd + 3 * m)

            def piece_b(hd, par_, c):
                cols = slice(c * CH, c * CH + CH)
                if c:
                    dve.wait_ge(half_done, J_B + hd + 1)
                else:
                    dve.wait_ge(chunk_done, 5 * HEADS_A + 3 * hd + 3)
                    dve.wait_ge(qk_ready, 2 * HEADS_A + hd)
                V.tensor_tensor(q_buf[0:QB, par_, cols], ps[0:QB, c, 0:CH], cos_t[0:QB, cols],
                                ALU.mult).then_inc(rot_step, 1)
                V.stream_shuffle(swapped[NOPE:QB, cols], ps[NOPE:QB, c, 0:CH], SWAP16).then_inc(chunk_taken, 1)
                if c:
                    dve.wait_ge(chunk_taken, 6 * HEADS_A + 2 * hd + 2)
                    rotate(slice(NOPE, QB), q_buf[NOPE:QB, par_, :], 6 * HEADS_A + 2 + 3 * hd)

            def unit_no(kind, hd, idx):
                return (5 * hd if kind == "A" else 5 * HEADS_A + 5 * hd) + idx

            def maximum(kind, hd, par_, idx):
                t, nq, _ = unit(idx)
                u, up, maps = unit_no(kind, hd, idx), (par_ + idx) % 2, 2 if kind == "A" else 1
                nk = META + P * t
                b = s_base(kind, idx, 0)
                dve.wait_ge(s_done, u + 1)
                if kind == "A":
                    both = flat[:, 1024:3072].rearrange("p (m c) -> p m c", m=2)[:, :, 512 - META:]
                else:
                    both = flat[:, b:b + nk].unsqueeze(1)
                if t:
                    V.memset(both[0:64, :, nk - 64:nk], NEG).then_inc(corner_set, 1)
                    dve.wait_ge(corner_set, (4 * hd if kind == "A" else 4 * HEADS_A + 4 * hd) + idx + 1)
                V.tensor_reduce(neg_max[0:nq, 2 * up:2 * up + maps], both[0:nq, :, 0:nk], AX.X, ALU.max,
                                negate=True).then_inc(max_done, 1)

            def combine(kind, hd, par_, idx):
                t, nq, _ = unit(idx)
                u, up, maps = unit_no(kind, hd, idx), (par_ + idx) % 2, 2 if kind == "A" else 1
                nk = META + P * t
                steps = 3 * u if kind == "A" else 15 * HEADS_A + 5 * hd + idx
                dve.wait_ge(exp_done, u + 1)
                rec = recips[0:nq, 2 * up:2 * up + maps]
                V.reciprocal(rec, sums[0:nq, 2 * up:2 * up + maps]).then_inc(comb_step, 1)
                dve.wait_ge(comb_step, steps + 1)
                p0, p1 = prob[0:nq, up, 0, 0:nk], prob[0:nq, up, 1, 0:nk]
                if kind == "B":
                    V.tensor_scalar(p0, p0, rec, None, ALU.mult).then_inc(a_ready, 1)
                    return
                V.tensor_scalar(rec[:, 1:2], rec[:, 1:2], neg_lam[0:nq, :], None, ALU.mult).then_inc(comb_step, 1)
                dve.wait_ge(comb_step, steps + 2)
                V.tensor_scalar(p1, p1, rec[:, 1:2], None, ALU.mult).then_inc(comb_step, 1)
                dve.wait_ge(comb_step, steps + 3)
                V.scalar_tensor_tensor(p0, p0, rec[:, 0:1], p1, ALU.mult, ALU.add).then_inc(a_ready, 1)

            def take_output(kind, hd, par_, idx, o_tile):
                t, nq, q0 = unit(idx)
                rows = slice(0, P) if kind == "A" else slice(64 * par_, 64 * par_ + 64)
                dve.wait_ge(pv_done, unit_no(kind, hd, idx) + 1)
                V.tensor_copy(o_buf[rows, o_tile, q0:q0 + nq], ps[rows, 7, P:P + nq]).then_inc(o_taken, 1)

            def head_a(hd, par_, more=True):
                def nxt(f, *a):
                    if more:
                        f(hd + 1, 1 - par_, *a)
                nxt(piece_a, 0)
                maximum("A", hd, par_, 1), combine("A", hd, par_, 1)
                nxt(piece_a, 1)
                take_output("A", hd, par_, 0, hd)
                maximum("A", hd, par_, 2), combine("A", hd, par_, 2)
                nxt(piece_a, 2)
                take_output("A", hd, par_, 1, hd)
                maximum("A", hd, par_, 3), combine("A", hd, par_, 3)
                nxt(piece_a, 3)
                take_output("A", hd, par_, 2, hd)
                maximum("A", hd, par_, 4), combine("A", hd, par_, 4)
                nxt(piece_a, 4)
                take_output("A", hd, par_, 3, hd)
                if more:
                    maximum("A", hd + 1, 1 - par_, 0), combine("A", hd + 1, 1 - par_, 0)
                nxt(piece_a, 5)
                take_output("A", hd, par_, 4, hd)

            def head_b(hd, par_, o_tile, more=True):
                def nxt(f, *a):
                    if more:
                        f(hd + 1, 1 - par_, *a)
                combine("B", hd, par_, 1)
                maximum("B", hd, par_, 2)
                take_output("B", hd, par_, 0, o_tile)
                combine("B", hd, par_, 2), maximum("B", hd, par_, 3)
                nxt(piece_b, 0)
                take_output("B", hd, par_, 1, o_tile)
                combine("B", hd, par_, 3), maximum("B", hd, par_, 4)
                nxt(piece_b, 1)
                take_output("B", hd, par_, 2, o_tile)
                combine("B", hd, par_, 4)
                take_output("B", hd, par_, 3, o_tile)
                if more:
                    maximum("B", hd + 1, 1 - par_, 0), maximum("B", hd + 1, 1 - par_, 1)
                    combine("B", hd + 1, 1 - par_, 0)
                take_output("B", hd, par_, 4, o_tile)
                if par_:
                    dve.wait_ge(o_taken, 5 * HEADS_A + 5 * hd + 5)
                    parts(o_buf[:, o_tile, :], g_hi[:, o_tile, :], g_lo[:, o_tile, :], gh_done, G_BO + o_tile,
                          g_ready)

            V.memset(ones[:, :], 1.0)
            V.memset(eps, EPS).then_inc(consts_set, 1)
            dve.wait_ge(par_loaded, 16)
            clear_acc(N_A)
            for m in range(KD):
                dve.wait_ge(x_loaded[m // 2], 16)
                scaled_operand(m, "a_attn_norm", X_A, T1)
                square_sum(m, N_A, T1)
            lam = par[:, PAR["lam"]:PAR["lam"] + 256].rearrange("p (a b d) -> p a b d", a=2, b=2)
            prod = swapped[:, 0:128].rearrange("p (a d) -> p a d", a=2)
            V.tensor_tensor(prod, lam[:, :, 0, :], lam[:, :, 1, :], ALU.mult).then_inc(lam_step, 1)
            dve.wait_ge(lam_step, 1)
            V.tensor_reduce(lam_dot, prod, AX.X, ALU.add).then_inc(lam_step, 1)
            V.tensor_scalar(sub_gain, pcol("a_sub"), 1.0 - LAM_INIT, None, ALU.mult).then_inc(lam_step, 1)
            dve.wait_ge(lam_exp_done, 1)
            V.scalar_tensor_tensor(neg_lam, lam_exp[:, 1:2], -LAM_INIT, lam_exp[:, 0:1], ALU.add,
                                   ALU.subtract).then_inc(lam_step, 1)
            dve.wait_ge(tab_loaded, 32)
            dve.wait_ge(r_ready, N_A + 1)
            V.tensor_tensor(cos_r, cos_t, r[:, :], ALU.mult).then_inc(tabs_made, 1)
            V.tensor_tensor(sin_r, sin_t, r[:, :], ALU.mult).then_inc(tabs_made, 1)
            dve.wait_ge(tabs_made, 2)
            dve.wait_ge(lam_step, 4)
            for p in range(6):
                piece_a(0, 0, p)
            maximum("A", 0, 0, 0), combine("A", 0, 0, 0)
            head_a(0, 0)
            with dve.Fori(0, (HEADS_A - 2) // 2) as i:
                for n in range(2):
                    head_a(2 * i + 1 + n, (1 + n) % 2)
            head_a(HEADS_A - 1, 1, more=False)
            dve.wait_ge(o_taken, 5 * HEADS_A)
            for n in range(HEADS_A):
                dve.wait_ge(r_ready, N_SUB + n + 1)
                V.scalar_tensor_tensor(o_buf[:, n, :], o_buf[:, n, :], sub_gain, (cos_r, sin_r)[n % 2],
                                       ALU.mult, ALU.mult).then_inc(sub_step, 1)
                dve.wait_ge(sub_step, n + 1)
                parts(o_buf[:, n, :], g_hi[:, n, :], g_lo[:, n, :], gh_done, G_WO + n, g_ready)
            residual(J_WO, TL_WO, T1, N_F0, "ffn_norm0", X_F0)
            ffn(J_F0, TL_F0, 0, G_F0, T1, N_F0, N_DD, "kv_norm", X_KV)

            dve.wait_ge(half_done, J_DD)
            for m in range(KD):
                g = pcol("b_attn_norm", m)
                V.tensor_scalar(g_hi[:, m, :], h[:, m, :], g, None, ALU.mult).then_inc(gh_done, 1)
                dve.wait_ge(gh_done, G_DQ + m + 1)
                V.scalar_tensor_tensor(g_lo[:, m, :], h[:, m, :], g, g_hi[:, m, :].bitcast(F32), ALU.mult,
                                       ALU.subtract).then_inc(g_ready, 1)
            dve.wait_ge(r_ready, N_DD + 1)
            dve.wait_ge(tab2_loaded, 32)
            rope = slice(NOPE, QB)
            V.tensor_tensor(cos_r[rope, :], cos_t[rope, :], r[rope, :], ALU.mult).then_inc(tabs_made, 1)
            V.tensor_tensor(sin_r[rope, :], sin_t[rope, :], r[rope, :], ALU.mult).then_inc(tabs_made, 1)
            dve.wait_ge(tabs_made, 4)

            def take_latent(m, i):
                dve.wait_ge(half_done, J_DD + m + 1)
                V.tensor_tensor(cut(latent[:, i, :], T1), result(J_DD + m, T1), cut(r[:, :], T1),
                                ALU.mult).then_inc(tile_taken, 1)

            def norm_latent(i, gain, rms, sem_value, count):
                dve.wait_ge(r_ready, sem_value)
                V.scalar_tensor_tensor(latent[:, i, :], latent[:, i, :], gain, rms, ALU.mult,
                                       ALU.mult).then_inc(lat_step, 1)
                dve.wait_ge(lat_step, i + 1)
                parts(latent[:, i, :], x_hi[:, i, :], x_lo[:, i, :], xh_done, X_CKV + count, x_ready)

            take_latent(0, 0), take_latent(1, 1)
            dve.wait_ge(half_done, J_DD + 3)
            V.stream_shuffle(cut(swapped[rope, :], T1), result(J_DD + 2, T1)[rope], SWAP16).then_inc(rot_step, 1)
            V.tensor_tensor(cut(k_buf[rope, 0, :], T1), result(J_DD + 2, T1)[rope], cut(cos_r[rope, :], T1),
                            ALU.mult).then_inc(tile_taken, 1)
            dve.wait_ge(rot_step, 6 * HEADS_A + 1)
            V.tensor_tensor(swapped[rope, :], swapped[rope, :], sin_r[rope, :], ALU.mult).then_inc(rot_step, 1)
            dve.wait_ge(rot_step, 6 * HEADS_A + 2)
            dve.wait_ge(tile_taken, TL_DD + 3)
            V.tensor_tensor(k_buf[rope, 0, :], k_buf[rope, 0, :], swapped[rope, :], ALU.add).then_inc(krope_step, 1)
            dve.wait_ge(krope_step, 1)
            V.tensor_copy(k_buf[rope, 1, :], k_buf[rope, 0, :]).then_inc(krope_step, 1)
            wait(dve, ss_ready, N_KV)
            dve.wait_ge(sq_ready, SQ[N_KV] + 2)
            V.tensor_tensor(acc[:, :], sq[:, 0, :], sq[:, 1, :], ALU.add).then_inc(acc_step, 1)
            take_latent(3, 2)
            take_latent(4, 3)
            take_latent(5, 4)
            wait(dve, ss_ready, N_KQ)
            dve.wait_ge(sq_ready, SQ[N_KQ] + 2)
            V.tensor_tensor(acc[:, :], sq[:, 0, :], sq[:, 1, :], ALU.add).then_inc(acc_step, 1)
            for i in range(KKV):
                norm_latent(i, pcol("kv_a", i), r_lat, N_KV + 1, i)
            dve.wait_ge(sq_ready, SQ[N_KQ] + 3)
            dve.wait_ge(acc_step, ACC[N_KQ] + 1)
            V.tensor_tensor(acc[:, :], acc[:, :], sq[:, 0, :], ALU.add).then_inc(acc_step, 1)
            for i in range(KQ):
                norm_latent(KKV + i, pcol("q_a", i), r[:, :], N_KQ + 1, KKV + i)

            piece_b(0, 0, 0), piece_b(0, 0, 1)
            maximum("B", 0, 0, 0), maximum("B", 0, 0, 1), combine("B", 0, 0, 0)
            head_b(0, 0, 0)
            with dve.Fori(0, 3) as i:
                for n in range(4):
                    head_b(4 * i + 1 + n, (1 + n) % 2, 2 * i + (1 + n) // 2)
            for n in range(13, HEADS_B):
                head_b(n, n % 2, n // 2, more=n < HEADS_B - 1)
            residual(J_BO, TL_BO, T1, N_BO, "ffn_norm1", X_F1)

            def turn_rest(src, dst, quarter, n):
                ops = [
                    lambda: V.tensor_scalar(turns, src, 1.0 / (2 * np.pi), quarter / 4.0, ALU.mult, ALU.add),
                    lambda: V.tensor_scalar(turns, turns, ROUND, None, ALU.add),
                    lambda: V.tensor_scalar(turns, turns, ROUND, None, ALU.subtract),
                    lambda: V.scalar_tensor_tensor(dst, turns, -TWO_PI_A, src, ALU.mult, ALU.add),
                    lambda: V.scalar_tensor_tensor(dst, turns, -TWO_PI_B, dst, ALU.mult, ALU.add),
                    lambda: V.scalar_tensor_tensor(dst, turns, -TWO_PI_C, dst, ALU.mult, ALU.add),
                    lambda: V.tensor_scalar(dst, dst, quarter * float(np.pi) / 2, None, ALU.add),
                    lambda: V.tensor_scalar(dst, dst, 3.1415925, -3.1415925, ALU.min, ALU.max)]
                for k, op in enumerate(ops):
                    dve.wait_ge(ang_step, n + k)
                    op().then_inc(ang_step, 1)

            dve.wait_ge(pos_loaded, 16)
            V.tensor_copy(pos_f, pos_i).then_inc(ang_step, 1)
            dve.wait_ge(ang_step, 1)
            V.tensor_scalar(ang, pos_f, cst[:, 3 * P:3 * P + 1], None, ALU.mult).then_inc(ang_step, 1)
            turn_rest(ang, red, 0, 2)
            turn_rest(ang, pos_f, 1, 10)
            dve.wait_ge(tab2_made, 2)
            V.tensor_scalar(sin2, sin2, cst[:, 3 * P + 1:3 * P + 2], None, ALU.mult).then_inc(ang_step, 1)
            ffn(J_F1, TL_F1, 1, G_F1, T1, N_BO, N_FIN1, Tn=T2)

            V.memset(mix_pad[:, 0:2], 0.0).then_inc(pads_set, 1)
            dve.wait_ge(r_ready, N_FIN1 + 1)
            clear_acc(N_MIX)
            for m in range(KD):
                hm = h[:, m, META:T1]
                V.scalar_tensor_tensor(hm, hm, pcol("final_norm", m), r[:, 0:T2], ALU.mult,
                                       ALU.mult).then_inc(h2_ready, 1)
                dve.wait_ge(h2_ready, m + 1)
                scaled_operand(m, "norm_mix", X_C, T2)
                if m:
                    square_sum(m - 1, N_MIX, T2)
            square_sum(KD - 1, N_MIX, T2)
            dve.wait_ge(r_ready, N_MIX + 1)
            dve.wait_ge(ang_step, 19)

            def rotate2(m):
                n = m if m < 2 else m - 1
                y = k2[:, m, :] if m < 2 else q2[:, m - 3, :]
                dve.wait_ge(y_ready, m + 1)
                wait(dve, k2q2_ready, n)
                V.stream_shuffle(swapped2, y, SWAP16).then_inc(rot2_step, 1)
                V.tensor_tensor(y, y, cos2, ALU.mult).then_inc(rot2_step, 1)
                dve.wait_ge(rot2_step, 3 * n + 1)
                V.tensor_tensor(swapped2, swapped2, sin2, ALU.mult).then_inc(rot2_step, 1)
                dve.wait_ge(rot2_step, 3 * n + 3)
                V.tensor_tensor(y, y, swapped2, ALU.add).then_inc(k2q2_ready, 1)

            def mix(jj, cx):
                w = PAR["conv_mix"] + jj
                if cx:
                    dve.wait_ge(y_ready, 9 + 3 * jj)
                    V.tensor_tensor(mix_pad[:, 2:], cc_val, cx_val, ALU.mult).then_inc(mix_step, 1)
                    dve.wait_ge(mix_step, 4 * jj + 1)
                    dve.wait_ge(mix_start, jj + 1)
                    for k in (1, 2):
                        V.scalar_tensor_tensor(mix_conv, mix_pad[:, k:k + T2], par[:, w + KD * k:w + KD * k + 1],
                                               mix_conv, ALU.mult, ALU.add).then_inc(mix_step, 1)
                        dve.wait_ge(mix_step, 4 * jj + 1 + k)
                else:
                    dve.wait_ge(y_ready, 10 + 3 * jj)
                    dve.wait_ge(g_ready, G_CO + jj)
                    V.tensor_tensor(mix_val, mix_conv, cb_val, ALU.mult).then_inc(mix_step, 1)
                    dve.wait_ge(mix_step, 4 * jj + 4)
                    parts(mix_val, g_hi[:, jj, 0:T2], g_lo[:, jj, 0:T2], gh_done, G_CO + jj, g_ready)

            def window_scores(u):
                g, n = divmod(u, 4)
                k0 = 0 if n else P
                dve.wait_ge(s2_done, u + 1)
                wait(dve, t2_done, u)
                s = flat[:, 2048:3072].rearrange("p (i k) -> p i k", i=4)[:, :, k0:]
                mask = cst[:, P + k0:3 * P].unsqueeze(1).to_broadcast([P, 4, 2 * P - k0])
                V.scalar_tensor_tensor(prob2[:, :, k0:], s, 0.125, mask, ALU.mult, ALU.add).then_inc(masked, 1)
                dve.wait_ge(masked, u + 1)
                V.tensor_reduce(max2, prob2[:, :, k0:], AX.X, ALU.max).then_inc(max2_step, 1)
                sink = par[:, PAR["sinks"] + 4 * g:PAR["sinks"] + 4 * g + 4]
                dve.wait_ge(max2_step, 4 * u + 1)
                V.tensor_tensor(max2, max2, sink, ALU.max).then_inc(max2_step, 1)
                dve.wait_ge(max2_step, 4 * u + 2)
                V.tensor_scalar(neg2, max2, -1.0, None, ALU.mult).then_inc(max2_step, 1)
                dve.wait_ge(max2_step, 4 * u + 3)
                V.tensor_tensor(sink_arg, sink, neg2, ALU.add).then_inc(max2_step, 1)

            def window_probs(u):
                n = u % 4
                k0 = 0 if n else P
                dve.wait_ge(exp2_done, u + 1)
                dve.wait_ge(sink_done, u + 1)
                V.tensor_tensor(den2, sum2, sink_exp, ALU.add).then_inc(den_step, 1)
                dve.wait_ge(den_step, 2 * u + 1)
                V.reciprocal(rec2, den2).then_inc(den_step, 1)
                dve.wait_ge(den_step, 2 * u + 2)
                V.tensor_tensor(prob2[:, :, k0:], prob2[:, :, k0:],
                                rec2.unsqueeze(2).to_broadcast([P, 4, 2 * P - k0]), ALU.mult).then_inc(p2_ready, 1)

            def window_output(u):
                g, n = divmod(u, 4)
                dve.wait_ge(pv2_done, u + 1)
                for e in range(2):
                    V.tensor_copy(o2[64 * e:64 * e + 64, 2 * g:2 * g + 2, n * P:n * P + P],
                                  ps[0:64, 1, 256 * e:256 * e + 256].rearrange("p (a q) -> p a q", a=2)
                                  ).then_inc(o2_taken, 1)

            for m in range(TILES_C + 1):
                for u in range(8):
                    if m == unit2_at(u) + 4:
                        window_output(u)
                    if m == unit2_at(u) + 1:
                        window_scores(u)
                if m < TILES_C:
                    dve.wait_ge(half_done, J_C + m + 1)
                    wait(dve, y_ready, m - 1)
                    V.tensor_tensor(y_val[:, m % 2, :], result(J_C + m, T2), r[:, 0:T2],
                                    ALU.mult).then_inc(tile_taken, 1)
                if m - 1 in (0, 1, 3, 4, 5, 6):
                    rotate2(m - 1)
                jj, part = divmod(m - 1 - 7, 3)
                if 0 <= jj < KD and part:
                    mix(jj, part == 1)
                for u in range(8):
                    if m == unit2_at(u) + 1:
                        window_probs(u)

            dve.wait_ge(half_done, J_CO)
            dve.wait_ge(o2_taken, 16)
            for g in range(4):
                parts(o2[:, g, :], x_hi[:, g, 0:T2], x_lo[:, g, 0:T2], xh_done, X_AO + g, x_ready)
            dve.wait_ge(y_ready, TILES_C)
            with dve.Fori(0, KD // 4) as i:
                for m in range(4):
                    dve.wait_ge(half_done, J_CO + m + 1 + 4 * i)
                    V.tensor_tensor(gates[:, m + 4 * i, :], result(J_CO + m, T2), gates[:, m + 4 * i, :],
                                    ALU.mult).then_inc(tile_taken, 1)
            dve.wait_ge(tile_taken, TL_AO)
            for m in range(KD):
                dve.wait_ge(half_done, J_AO + m + 1)
                V.scalar_tensor_tensor(y_val[:, m % 2, :], result(J_AO + m, T2), pcol("b_attn_out", m),
                                       gates[:, KD + m, :], ALU.add, ALU.mult).then_inc(tile_taken, 1)
                dve.wait_ge(tile_taken, TL_AO + m + 1)
                dve.wait_ge(g_ready, G_MX + m)
                V.tensor_tensor(mix_val, y_val[:, m % 2, :], gates[:, m, :], ALU.add).then_inc(merge_step, 1)
                dve.wait_ge(merge_step, m + 1)
                parts(mix_val, g_hi[:, m, 0:T2], g_lo[:, m, 0:T2], gh_done, G_MX + m, g_ready)
            residual(J_MX, TL_MX, T2, N_F2, "norm_ffn2", X_F2)
            ffn(J_F2, TL_F2, 2, G_F2, T2, N_F2, N_FIN2)
            dve.wait_ge(r_ready, N_FIN2 + 1)
            for m in range(KD):
                hm = h[:, m, META:T1]
                V.scalar_tensor_tensor(hm, hm, pcol("final_norm2", m), r[:, 0:T2], ALU.mult,
                                       ALU.mult).then_inc(fin_ready, 1)

        @block.scalar
        def _(act):
            A = nc.scalar

            act.dma_start(par[:, :], params).then_inc(par_loaded, 16)
            act.dma_start(cst[:, :], consts_dram).then_inc(cst_loaded, 16)
            act.dma_start(cos_t, tabs_dram[0]).then_inc(tab_loaded, 16)
            act.dma_start(sin_t, tabs_dram[1]).then_inc(tab_loaded, 16)

            def hi_part(j, i=0, stride=4):
                if isinstance(j, int) and j >= HALVES:
                    return
                act.wait_ge(raw_loaded[j % 4], 16 * (j // 4 + 1) + 4 * stride * i)
                wait(act, half_done, j - 3 + stride * i)
                A.activation(w_hi[:, j % 4, :], w_raw[:, j % 4, :], ACT.Copy).then_inc(hi_ready, 1)

            def square(src, k, sq0, taken, steps, T, i=0):
                act.wait_ge(*taken)
                wait(act, *steps)
                A.activation(sq[:, k % 2, 0:T], src, ACT.Square).then_inc(sq_ready, 1)

            def inverse_rms(norm, features, T, dst, bank0=6):
                act.wait_ge(ss_ready, norm + 1)
                src = ps[:, bank0:bank0 + 2, 0:CH] if T == T1 else ps[:, bank0, 0:T2]
                A.activation(cut(dst[:, 0:T], T), src, ACT.Ln, bias=eps, scale=1.0 / features).then_inc(ln_done, 1)
                act.wait_ge(ln_done, norm + 1)
                A.activation(dst[:, 0:T], dst[:, 0:T], ACT.Exp, scale=-0.5).then_inc(r_ready, 1)

            def residual(j, tl, T, norm=None):
                if j + KD + 3 <= HALVES:
                    with act.Fori(0, KD // 4) as i:
                        for m in range(4):
                            hi_part(j + m + 3, i)
                            if norm is not None:
                                square(h[:, m + 4 * i, tok(T)], m, SQ[norm], (tile_taken, tl + m + 1 + 4 * i),
                                       (acc_step, ACC[norm] + m + 4 * i), T)
                else:
                    for m in range(KD):
                        hi_part(j + m + 3)
                        if norm is not None:
                            square(h[:, m, tok(T)], m, SQ[norm], (tile_taken, tl + m + 1),
                                   (acc_step, ACC[norm] + m), T)

            def ffn(j, tl, layer, T, norm, norm_next, Tn=None):
                f, pair0 = 0, FF * layer
                for n, g in enumerate(GROUPS):
                    if n == 0:
                        inverse_rms(norm, D, T, r)
                        act.wait_ge(hid_step, pair0 + layer + 1)
                    with act.Fori(0, g // 2) as i:
                        for q in range(2):
                            jq, pair = j + 2 * q, pair0 + f + q
                            hi_part(jq + 3, i)
                            o, b = PAR[f"conv{layer}"] + f + q, PAR[f"convb{layer}"] + f + q
                            act.wait_ge(tile_taken, tl + 2 * q + 1 + 4 * i)
                            A.activation(conv[:, 0:T], a_pad[:, 0:T], ACT.Identity,
                                         bias=par[:, bass.ds(b + 2 * i, 1)],
                                         scale=par[:, bass.ds(o + 2 * i, 1)]).then_inc(conv_start, 1)
                            act.wait_ge(conv_step, 2 * pair + 2 + 4 * i)
                            act.wait_ge(hid_step, pair + layer + 1 + 2 * i)
                            A.activation(silu[:, 0:T], conv[:, 0:T], ACT.Silu).then_inc(silu_ready, 1)
                            hi_part(jq + 4, i)
                    j, tl, f = j + 2 * g, tl + 2 * g, f + g
                    residual(j, tl, Tn or T, norm_next if n == len(GROUPS) - 1 else None)
                    j, tl = j + KD, tl + KD

            def unit_no(kind, hd, idx):
                return (5 * hd if kind == "A" else 5 * HEADS_A + 5 * hd) + idx

            def exps(kind, hd, par_, idx):
                t, nq, _ = unit(idx)
                u, up, nk = unit_no(kind, hd, idx), (par_ + idx) % 2, META + P * t
                act.wait_ge(max_done, u + 1)
                wait(act, t_done, u - 1)
                for m in range(2 if kind == "A" else 1):
                    b = s_base(kind, idx, m)
                    c = 2 * up + m
                    last = A.activation(prob[0:nq, up, m, 0:nk], flat[0:nq, b:b + nk], ACT.Exp,
                                        bias=neg_max[0:nq, c:c + 1], accum_out=sums[0:nq, c:c + 1])
                last.then_inc(exp_done, 1)

            def take_transposed(kind, hd, par_, idx):
                t, nq, _ = unit(idx)
                u, up = unit_no(kind, hd, idx), (par_ + idx) % 2
                act.wait_ge(t_done, u + 1)
                wait(act, pv_done, u - 1)
                if t:
                    A.activation(pt[:, up, 0:t * P], ps[:, 6, 0:t * P], ACT.Copy)
                bank, c = (7, 0) if t == 4 else (6, t * P)
                A.activation(pt_meta[0:META, up, 0:nq], ps[0:META, bank, c:c + nq], ACT.Copy).then_inc(pt_ready, 1)

            def take_values(kind, hd, par_):
                w = P if kind == "A" else 64
                four = ps[:, 6, :].rearrange("p (b n) -> p b n", b=4)[:, :, P - w:]
                act.wait_ge(vt_done, (hd if kind == "A" else HEADS_A + hd) + 1)
                A.activation(v_tok[:, par_, 0:4 * w].rearrange("p (b n) -> p b n", b=4), four, ACT.Copy)
                A.activation(v_meta[0:META, par_, 0:w], ps[0:META, 7, P - w:P], ACT.Copy).then_inc(v_ready, 1)

            def head_a(hd, par_, j, i=0, more=True):
                def hi_next(n):
                    if more:
                        hi_part(j + 3 + n, i, 8)
                take_values("A", hd, par_)
                take_transposed("A", hd, par_, 0)
                hi_next(0)
                exps("A", hd, par_, 1), take_transposed("A", hd, par_, 1)
                exps("A", hd, par_, 2)
                hi_next(1)
                take_transposed("A", hd, par_, 2), exps("A", hd, par_, 3)
                take_transposed("A", hd, par_, 3), exps("A", hd, par_, 4)
                hi_next(2)
                take_transposed("A", hd, par_, 4)
                if more:
                    exps("A", hd + 1, 1 - par_, 0)
                hi_next(3)

            def keys_values(hd, par_, c):
                cols = slice(c * CH, c * CH + CH)
                act.wait_ge(chunk_done, 5 * HEADS_A + 3 * hd + c + 1)
                A.activation(k_buf[0:NOPE, par_, cols], ps[0:NOPE, c, 0:CH], ACT.Copy, scale=96.0 ** -0.25)
                A.activation(vt_buf[NOPE:P, cols], ps[NOPE:P, c, 0:CH], ACT.Copy).then_inc(kv_taken, 1)

            def head_b(hd, par_, j, i=0, more=True):
                take_values("B", hd, par_)
                if more:
                    hi_part(j + 3, i)
                    keys_values(hd + 1, 1 - par_, 0)
                take_transposed("B", hd, par_, 0), exps("B", hd, par_, 2)
                if more:
                    keys_values(hd + 1, 1 - par_, 1)
                take_transposed("B", hd, par_, 1), exps("B", hd, par_, 3)
                take_transposed("B", hd, par_, 2), exps("B", hd, par_, 4)
                take_transposed("B", hd, par_, 3)
                take_transposed("B", hd, par_, 4)
                if more:
                    exps("B", hd + 1, 1 - par_, 0), exps("B", hd + 1, 1 - par_, 1)

            act.wait_ge(consts_set, 1)
            for m in range(KD):
                square(h[:, m, :], m, 0, (x_loaded[m // 2], 16), (acc_step, m), T1)
                if m in (1, 3, 5):
                    hi_part(m // 2)
            act.wait_ge(lam_step, 2)
            A.activation(lam_exp, lam_dot, ACT.Exp).then_inc(lam_exp_done, 1)
            inverse_rms(N_A, D, T1, r)
            for j in range(3, 7):
                hi_part(j)
            exps("A", 0, 0, 0)
            head_a(0, 0, 4)
            with act.Fori(0, (HEADS_A - 2) // 2) as i:
                for n in range(2):
                    head_a(2 * i + 1 + n, (1 + n) % 2, 8 + 4 * n, i)
            head_a(HEADS_A - 1, 1, 0, more=False)
            act.wait_ge(tabs_made, 2)
            act.dma_start(cos_t, tabs_dram[2]).then_inc(tab2_loaded, 16)
            act.dma_start(sin_t, tabs_dram[3]).then_inc(tab2_loaded, 16)
            for n in range(HEADS_A + 1):
                if n < HEADS_A:
                    square(o_buf[:, n, :], n, 0, (o_taken, 5 * n + 5), (ss_ready, N_SUB + n - 1), T1)
                if n:
                    wait(act, sub_step, n - 2)
                    inverse_rms(N_SUB + n - 1, P, T1, (cos_r, sin_r)[(n - 1) % 2], 4 + 2 * ((n - 1) % 2))
            residual(J_WO, TL_WO, T1, N_F0)
            ffn(J_F0, TL_F0, 0, T1, N_F0, N_DD)
            hi_part(J_DD + 3)
            inverse_rms(N_DD, D, T1, r)
            for m, k in ((0, 0), (1, 1), (2, None), (3, 2), (4, 3), (5, 4)):
                if m:
                    hi_part(J_DD + m + 3)
                if k is not None:
                    norm = N_KV if k < KKV else N_KQ
                    kk = k if k < KKV else k - KKV
                    free = ACC[N_KV] if k < KKV else ACC[N_KQ] + (kk == 2)
                    square(latent[:, k, :], kk, 0, (tile_taken, TL_DD + m + 1), (acc_step, free), T1)
                if m == 3:
                    inverse_rms(N_KV, KKV * P, T1, r_lat)
            inverse_rms(N_KQ, KQ * P, T1, r)
            act.wait_ge(lat_step, KKV)
            hi_part(J_B + 3)
            keys_values(0, 0, 0), keys_values(0, 0, 1)
            exps("B", 0, 0, 0), exps("B", 0, 0, 1)
            head_b(0, 0, J_B + 1)
            with act.Fori(0, 3) as i:
                for n in range(4):
                    head_b(4 * i + 1 + n, (1 + n) % 2, J_B + 2 + n, i)
            for n in range(13, HEADS_B):
                head_b(n, n % 2, J_B + n + 1, more=n < HEADS_B - 1)
            act.wait_ge(o_taken, 5 * (HEADS_A + HEADS_B))
            act.dma_start(pos_i, positions).then_inc(pos_loaded, 16)
            residual(J_BO, TL_BO, T1, N_BO)
            act.wait_ge(ang_step, 18)
            A.activation(sin2, red, ACT.Sin).then_inc(tab2_made, 1)
            A.activation(cos2, pos_f, ACT.Sin).then_inc(tab2_made, 1)
            ffn(J_F1, TL_F1, 1, T1, N_BO, N_FIN1, Tn=T2)
            inverse_rms(N_FIN1, D, T2, r)
            for m in range(KD):
                square(h[:, m, META:T1], m, 0, (h2_ready, m + 1), (acc_step, ACC[N_MIX] + m), T2)
            for m in range(TILES_C):
                hi_part(J_C + m + 3)
                if m == 0:
                    inverse_rms(N_MIX, D, T2, r)
                for u in range(8):
                    if m == unit2_at(u) + 3:
                        act.wait_ge(t2_done, u + 1)
                        wait(act, pv2_done, u)
                        kb = 0 if u % 4 else 1
                        A.activation(pt2[:, kb:, :], ps[:, 6 + kb:8, :], ACT.Copy).then_inc(pt2_ready, 1)
                    if m == unit2_at(u) + 1:
                        k0 = 0 if u % 4 else P
                        act.wait_ge(max2_step, 4 * u + 4)
                        for i in range(4):
                            last = A.activation(prob2[:, i, k0:], prob2[:, i, k0:], ACT.Exp, bias=neg2[:, i:i + 1],
                                                accum_out=sum2[:, i:i + 1])
                        last.then_inc(exp2_done, 1)
                        A.activation(sink_exp, sink_arg, ACT.Exp).then_inc(sink_done, 1)
                if m == 5:
                    act.wait_ge(vt2_done, 1)
                    A.activation(v2, ps[:, 3, :].rearrange("p (b n) -> p b n", b=4), ACT.Copy).then_inc(v2_ready, 1)
                jj, part = divmod(m - 7, 3)
                func = ACT.Identity
                if m < 2:
                    dst = k2[:, m, :]
                elif m == 2:
                    dst = vt2
                elif m < 7:
                    dst = q2[:, m - 3, :]
                elif jj < KD:
                    dst = (cc_val, cx_val, cb_val)[part]
                    wait(act, mix_step, 4 * jj - 3 if part < 2 else 4 * jj)
                else:
                    dst, func = gates[:, m - 7 - 3 * KD, :], ACT.Sigmoid
                act.wait_ge(tile_taken, TL_C + m + 1)
                A.activation(dst, y_val[:, m % 2, :], func, bias=pcol("b_in", m)).then_inc(y_ready, 1)
                if 0 <= jj < KD and part == 1:
                    act.wait_ge(mix_step, 4 * jj + 1)
                    act.wait_ge(pads_set, 1)
                    A.activation(mix_conv, mix_pad[:, 0:T2], ACT.Copy, scale=pcol("conv_mix", jj)
                                 ).then_inc(mix_start, 1)
            residual(J_CO, TL_CO, T2)
            residual(J_AO, TL_AO, T2)
            residual(J_MX, TL_MX, T2, N_F2)
            ffn(J_F2, TL_F2, 2, T2, N_F2, N_FIN2)
            inverse_rms(N_FIN2, D, T2, r)


def pack_half(*blocks):
    out = np.zeros((P, HW), np.float32)
    for n, b in enumerate(blocks):
        out[:b.shape[0], n * P:n * P + b.shape[1]] = b
    return out


def column_tiles(w, cols=None):
    rows = w.shape[0] // P
    return [pack_half(*(w[k * P:(k + 1) * P, c:c + P] for k in range(rows)))
            for c in (range(0, w.shape[1], P) if cols is None else cols)]


def ffn_halves(w_in, w_out):
    halves, f0 = [], 0
    for g in GROUPS:
        for f in range(f0, f0 + g):
            halves += column_tiles(w_in, (f * P, (FF + f) * P))
        halves += column_tiles(w_out[f0 * P:(f0 + g) * P])
        f0 += g
    return halves


def head_order2():
    return [16 * (n // 32) + n % 16 + (32 if n % 32 >= 16 else 0) for n in range(64)]


def input_columns2():
    cb, cc, cx, q, k, v, gc, ga = 0, 1024, 2048, 3072, 3584, 3712, 3840, 4864
    perm = np.array(head_order2())
    cols = [np.concatenate([k + 64 * g + perm] * 2) for g in range(2)]
    cols.append(v + np.arange(P))
    cols += [np.concatenate([q + 64 * (2 * t) + perm, q + 64 * (2 * t + 1) + perm]) for t in range(4)]
    for t in range(KD):
        cols += [o + P * t + np.arange(P) for o in (cc, cx, cb)]
    cols += [o + P * t + np.arange(P) for o in (gc, ga) for t in range(KD)]
    return np.concatenate(cols)


def weight_stream(i):
    qkv = i["a_w_qkv"][0]
    halves = []
    for hd in range(HEADS_A):
        blocks = [qkv[k * P:(k + 1) * P, D * part + P * hd:D * part + P * hd + P]
                  for part in (1, 0, 2) for k in range(KD)]
        halves += [pack_half(*blocks[6 * n:6 * n + 6]) for n in range(4)]
    halves += column_tiles(i["a_w_o"][0])
    halves += ffn_halves(i["ffn_w_in"][0], i["ffn_w_out"][0])
    dkv = i["kv_w_dkv"]
    rope_key = np.zeros((D, P), np.float32)
    rope_key[:, NOPE:QB] = dkv[:, KKV * P:]
    halves += column_tiles(dkv, range(0, KKV * P, P)) + column_tiles(rope_key) + column_tiles(i["b_w_dq"][0])
    ukv, uq = i["kv_w_ukv"], i["b_w_uq"][0]
    for hd in range(HEADS_B):
        halves.append(pack_half(*(ukv[k * P:(k + 1) * P, P * hd:P * hd + P] for k in range(KKV)),
                                *(uq[k * P:(k + 1) * P, QB * hd:QB * hd + QB] for k in range(KQ))))
    halves += column_tiles(i["b_w_o"][0])
    halves += ffn_halves(i["ffn_w_in"][1], i["ffn_w_out"][1])
    halves += column_tiles(i["w_in_2"][0][:, input_columns2()])
    halves += column_tiles(i["w_conv_out_2"][0]) + column_tiles(i["w_attn_out_2"][0])
    halves += column_tiles(i["w_mix_out_2"][0])
    halves += ffn_halves(i["w_ffn_up_2"][0], i["w_ffn_down_2"][0])
    assert len(halves) == HALVES
    return np.stack(halves)


def parameters(i):
    def tiles_of(v):
        return np.ascontiguousarray(v.reshape(-1, P).T)

    def rows(v):
        return np.broadcast_to(v.reshape(1, -1), (P, v.size))
    sinks = i["sinks_2"][0].reshape(2, 2, 2).transpose(0, 2, 1)
    lam = np.concatenate([i["a_lambda_q1"][0], i["a_lambda_k1"][0], i["a_lambda_q2"][0], i["a_lambda_k2"][0]])
    values = {
        "a_attn_norm": tiles_of(i["a_attn_norm"][0]), "ffn_norm0": tiles_of(i["ffn_norm"][0]),
        "kv_norm": tiles_of(i["kv_norm"]), "b_attn_norm": tiles_of(i["b_attn_norm"][0]),
        "ffn_norm1": tiles_of(i["ffn_norm"][1]), "final_norm": tiles_of(i["final_norm"]),
        "norm_mix": tiles_of(i["norm_mix_w_2"][0]), "norm_ffn2": tiles_of(i["norm_ffn_w_2"][0]),
        "final_norm2": tiles_of(i["norm_final_w_2"]), "a_sub": tiles_of(i["a_sub_norm"][0]),
        "kv_a": tiles_of(i["kv_a_norm"]), "q_a": tiles_of(i["b_q_a_norm"][0]),
        "conv0": tiles_of(i["ffn_conv_w"][0]), "convb0": tiles_of(i["ffn_conv_b"][0]),
        "conv1": tiles_of(i["ffn_conv_w"][1]), "convb1": tiles_of(i["ffn_conv_b"][1]),
        "conv2": tiles_of(i["ffn_conv_w_2"][0]), "convb2": tiles_of(i["ffn_conv_b_2"][0]),
        "conv_mix": tiles_of(i["conv_mix_w_2"][0]), "b_in": tiles_of(i["b_in_2"][0][input_columns2()]),
        "b_attn_out": tiles_of(i["b_attn_out_2"][0]), "sinks": rows(sinks), "lam": rows(lam)}
    return np.concatenate([values[name] for name, _ in PAR_SIZES], axis=1)


def layout(inputs):
    i = {name: np.asarray(a) for name, a in inputs.items()}
    tokens = np.concatenate([i["meta_tokens"], i["x"][0]], axis=0)
    return {
        "x_t": np.ascontiguousarray(tokens.T.reshape(KD, P, T1).transpose(1, 0, 2)),
        "stream": weight_stream(i),
        "params": np.ascontiguousarray(parameters(i)),
        "positions": np.ascontiguousarray(np.broadcast_to(i["positions_2"], (P, T2))),
    }


def kernel(**inputs):
    import concourse.bacc as bacc
    from concourse.bass_utils import run_bass_kernel_spmd

    nc = bacc.Bacc("TRN2", target_bir_lowering=False, num_devices=1)
    arrays = layout(inputs)
    args = [nc.dram_tensor(name, a.shape, mybir.dt.from_np(a.dtype), kind="ExternalInput").ap()
            for name, a in arrays.items()]
    args.append(nc.dram_tensor("out_t", (P, KD, T2), F32, kind="ExternalOutput").ap())
    program(nc, *args)
    result = run_bass_kernel_spmd(nc, [arrays], core_ids=[0]).results[0]["out_t"]
    return np.ascontiguousarray(result.transpose(2, 1, 0).reshape(1, T2, D))
```
